# Optimizing a Trainium2 kernel written in Bass

```python
import math
import jax
import jax.numpy as jnp
from jax import lax
import numpy as np

D_MODEL = 1024
BATCH = 1
SEQ = 512
DEPTH = 1
DEC_BATCH = 8
DEC_SEQ = 16
PAST_LEN = 1024

CHUNK = 64
CONV_W = 4
LRU_WIDTH = 1024
LRU_HEADS = 8
LRU_BLOCK = LRU_WIDTH // LRU_HEADS
LRU_C = 8.0
D_INNER = 2 * D_MODEL
SSD_HEAD_DIM = 64
SSD_HEADS = D_INNER // SSD_HEAD_DIM
SSD_GROUPS = 4
HEADS_PER_GROUP = SSD_HEADS // SSD_GROUPS
D_STATE = 128
SSD_CONV_DIM = D_INNER + 2 * SSD_GROUPS * D_STATE
N_BRANCH = 2
FFN_DIM = 2816
EPS = 1e-6
IN_COLS = 2 * LRU_WIDTH + D_INNER + SSD_CONV_DIM + SSD_HEADS + N_BRANCH * D_MODEL

kernel_name = 'hybrid_rglru_ssd_macaron_stream_step'

def _rmsnorm(x, g):
    xf = x.astype(jnp.float32)
    inv = lax.rsqrt(jnp.mean(xf * xf, axis=-1, keepdims=True) + EPS)
    return (xf * inv).astype(x.dtype) * g

def _swiglu(x, w_up, w_down):
    gate, up = jnp.split(x @ w_up, 2, axis=-1)
    return (jax.nn.silu(gate) * up) @ w_down

def _causal_conv(x, buf, w, b):
    L = x.shape[1]
    xp = jnp.concatenate([buf, x], axis=1)
    y = b + xp[:, 0:L, :] * w[0]
    for k in range(1, CONV_W):
        y = y + xp[:, k:k + L, :] * w[k]
    return y, xp[:, L:, :]

def _rglru(x, h0, w_rg, b_rg, w_ig, b_ig, lam):
    nb, L, _ = x.shape
    xb = x.reshape(nb, L, LRU_HEADS, LRU_BLOCK)
    r = jax.nn.sigmoid(jnp.einsum('blhi,hij->blhj', xb, w_rg).reshape(nb, L, LRU_WIDTH) + b_rg)
    i = jax.nn.sigmoid(jnp.einsum('blhi,hij->blhj', xb, w_ig).reshape(nb, L, LRU_WIDTH) + b_ig)
    log_a = -LRU_C * r.astype(jnp.float32) * jax.nn.softplus(-lam.astype(jnp.float32))
    a = jnp.exp(log_a)
    u = jnp.sqrt(-jnp.expm1(2.0 * log_a)) * (i * x).astype(jnp.float32)
    u = u.at[:, 0].add(a[:, 0] * h0.astype(jnp.float32))

    def combine(left, right):
        a1, b1 = left
        a2, b2 = right
        return a1 * a2, a2 * b1 + b2

    _, h = lax.associative_scan(combine, (a, u), axis=1)
    return h.astype(x.dtype), h[:, -1].astype(x.dtype)

def _segsum(x):
    T = x.shape[-1]
    xr = jnp.broadcast_to(x[..., :, None], x.shape + (T,))
    strict = jnp.tril(jnp.ones((T, T), dtype=bool), -1)
    cs = jnp.cumsum(jnp.where(strict, xr, 0.0), axis=-2)
    return jnp.where(jnp.tril(jnp.ones((T, T), dtype=bool)), cs, -jnp.inf)

def _ssd_scan(x, dt, A, Bm, Cm, h0):
    nb, L = x.shape[0], x.shape[1]
    cs = min(CHUNK, L)
    nc = L // cs
    G, E, P, N = SSD_GROUPS, HEADS_PER_GROUP, SSD_HEAD_DIM, D_STATE
    x = x.reshape(nb, nc, cs, G, E, P)
    dt = dt.reshape(nb, nc, cs, G, E)
    Bm = Bm.reshape(nb, nc, cs, G, N)
    Cm = Cm.reshape(nb, nc, cs, G, N)
    dA = jnp.moveaxis(dt * A.reshape(G, E), 2, -1)
    xd = x * dt[..., None]
    A_cs = jnp.cumsum(dA, axis=-1)
    Lmat = jnp.exp(_segsum(dA))
    CB = jnp.einsum('bclgn,bcsgn->bcgls', Cm, Bm)
    y_diag = jnp.einsum('bcgls,bcgels,bcsgep->bclgep', CB, Lmat, xd)
    decay_states = jnp.exp(A_cs[..., -1:] - A_cs)
    states = jnp.einsum('bcsgn,bcges,bcsgep->bcgepn', Bm, decay_states, xd)
    states = jnp.concatenate([h0.reshape(nb, G, E, P, N)[:, None], states], axis=1)
    chunk_decay = jnp.pad(A_cs[..., -1], ((0, 0), (1, 0), (0, 0), (0, 0)))
    decay_chunk = jnp.exp(_segsum(jnp.moveaxis(chunk_decay, 1, -1)))
    new_states = jnp.einsum('bgezc,bcgepn->bzgepn', decay_chunk, states)
    states_in, final = new_states[:, :-1], new_states[:, -1]
    y_off = jnp.einsum('bclgn,bcgepn,bcgel->bclgep', Cm, states_in, jnp.exp(A_cs))
    y = (y_diag + y_off).reshape(nb, L, SSD_HEADS, P)
    return y, final.reshape(nb, SSD_HEADS, P, N)

def _mixer(u, lru_conv_buf, lru_h0, ssd_conv_buf, ssd_h0, p):
    nb, L, _ = u.shape
    proj = u @ p['w_in']
    sizes = [LRU_WIDTH, LRU_WIDTH, D_INNER, SSD_CONV_DIM, SSD_HEADS, N_BRANCH * D_MODEL]
    offs = np.cumsum(sizes)[:-1].tolist()
    lru_x, lru_gate, z, xbc, dt_raw, gate_logits = jnp.split(proj, offs, axis=-1)

    xc, lru_conv_new = _causal_conv(lru_x, lru_conv_buf, p['lru_conv_w'], p['lru_conv_b'])
    h, lru_h_new = _rglru(xc, lru_h0, p['lru_w_rg'], p['lru_b_rg'], p['lru_w_ig'], p['lru_b_ig'], p['lru_lambda'])
    y_lru = jax.nn.gelu(lru_gate) * h

    xbc_c, ssd_conv_new = _causal_conv(xbc, ssd_conv_buf, p['ssd_conv_w'], p['ssd_conv_b'])
    xbc_c = jax.nn.silu(xbc_c)
    xs, Bm, Cm = jnp.split(xbc_c, [D_INNER, D_INNER + SSD_GROUPS * D_STATE], axis=-1)
    xs_h = xs.reshape(nb, L, SSD_HEADS, SSD_HEAD_DIM).astype(jnp.float32)
    dt = jax.nn.softplus(dt_raw.astype(jnp.float32) + p['ssd_dt_bias'].astype(jnp.float32))
    A = -jnp.exp(p['ssd_A_log'].astype(jnp.float32))
    y, ssd_h_new = _ssd_scan(
        xs_h, dt, A,
        Bm.reshape(nb, L, SSD_GROUPS, D_STATE).astype(jnp.float32),
        Cm.reshape(nb, L, SSD_GROUPS, D_STATE).astype(jnp.float32),
        ssd_h0.astype(jnp.float32))
    y = y + p['ssd_D'].astype(jnp.float32)[:, None] * xs_h
    y = y.reshape(nb, L, D_INNER).astype(u.dtype) * jax.nn.silu(z)
    y = _rmsnorm(y.reshape(nb, L, SSD_GROUPS, D_INNER // SSD_GROUPS),
                 p['ssd_norm_g'].reshape(SSD_GROUPS, D_INNER // SSD_GROUPS)).reshape(nb, L, D_INNER)

    g_lru, g_ssd = jnp.split(jax.nn.sigmoid(gate_logits + p['b_gate']), 2, axis=-1)
    m = g_lru * (y_lru @ p['w_br_lru']) + g_ssd * (y @ p['w_br_ssd'])
    out = m @ p['w_out']
    return out, lru_conv_new, lru_h_new, ssd_conv_new, ssd_h_new.astype(u.dtype)

def _layer(x, lru_conv_buf, lru_h0, ssd_conv_buf, ssd_h0, p):
    x = x + 0.5 * _swiglu(_rmsnorm(x, p['norm_ffn1_g']), p['ffn1_w_up'], p['ffn1_w_down'])
    mix, lcv, lh, scv, sh = _mixer(_rmsnorm(x, p['norm_mix_g']), lru_conv_buf, lru_h0, ssd_conv_buf, ssd_h0, p)
    x = x + mix
    x = x + 0.5 * _swiglu(_rmsnorm(x, p['norm_ffn2_g']), p['ffn2_w_up'], p['ffn2_w_down'])
    return x, (lcv, lh, scv, sh)

def setup_inputs(seed: int = 0) -> dict:
    key = jax.random.key(seed)
    ks = jax.random.split(key, 40)
    f32 = jnp.float32

    def nrm(k, shape, scale):
        return jax.random.normal(k, shape, f32) * scale

    u_lam = jax.random.uniform(ks[10], (DEPTH, LRU_WIDTH), f32, minval=0.9, maxval=0.999)
    dt0 = jnp.exp(jax.random.uniform(ks[14], (DEPTH, SSD_HEADS), f32,
                                     minval=math.log(1e-3), maxval=math.log(1e-1)))
    return {
        'x_prompt': nrm(ks[0], (BATCH, SEQ, D_MODEL), 1.0),
        'x_sample': nrm(ks[1], (DEC_BATCH, DEC_SEQ, D_MODEL), 1.0),
        'state_lru_conv': nrm(ks[2], (DEPTH, DEC_BATCH, CONV_W - 1, LRU_WIDTH), 1.0),
        'state_lru_h': nrm(ks[3], (DEPTH, DEC_BATCH, LRU_WIDTH), 0.5),
        'state_ssd_conv': nrm(ks[4], (DEPTH, DEC_BATCH, CONV_W - 1, SSD_CONV_DIM), 1.0),
        'state_ssd_h': nrm(ks[5], (DEPTH, DEC_BATCH, SSD_HEADS, SSD_HEAD_DIM, D_STATE), 0.1),
        'norm_ffn1_g': 1.0 + nrm(ks[6], (DEPTH, D_MODEL), 0.02),
        'ffn1_w_up': nrm(ks[7], (DEPTH, D_MODEL, 2 * FFN_DIM), D_MODEL ** -0.5),
        'ffn1_w_down': nrm(ks[8], (DEPTH, FFN_DIM, D_MODEL), FFN_DIM ** -0.5),
        'norm_mix_g': 1.0 + nrm(ks[9], (DEPTH, D_MODEL), 0.02),
        'w_in': nrm(ks[11], (DEPTH, D_MODEL, IN_COLS), D_MODEL ** -0.5),
        'b_gate': nrm(ks[12], (DEPTH, N_BRANCH * D_MODEL), 0.01),
        'lru_conv_w': nrm(ks[13], (DEPTH, CONV_W, LRU_WIDTH), CONV_W ** -0.5),
        'lru_conv_b': nrm(ks[15], (DEPTH, LRU_WIDTH), 0.01),
        'lru_w_rg': nrm(ks[16], (DEPTH, LRU_HEADS, LRU_BLOCK, LRU_BLOCK), LRU_BLOCK ** -0.5),
        'lru_b_rg': nrm(ks[17], (DEPTH, LRU_WIDTH), 0.01),
        'lru_w_ig': nrm(ks[18], (DEPTH, LRU_HEADS, LRU_BLOCK, LRU_BLOCK), LRU_BLOCK ** -0.5),
        'lru_b_ig': nrm(ks[19], (DEPTH, LRU_WIDTH), 0.01),
        'lru_lambda': jnp.log(u_lam) - jnp.log1p(-u_lam),
        'ssd_conv_w': nrm(ks[20], (DEPTH, CONV_W, SSD_CONV_DIM), CONV_W ** -0.5),
        'ssd_conv_b': nrm(ks[21], (DEPTH, SSD_CONV_DIM), 0.01),
        'ssd_dt_bias': dt0 + jnp.log(-jnp.expm1(-dt0)),
        'ssd_A_log': jnp.log(jax.random.uniform(ks[22], (DEPTH, SSD_HEADS), f32, minval=1.0, maxval=16.0)),
        'ssd_D': 1.0 + nrm(ks[23], (DEPTH, SSD_HEADS), 0.02),
        'ssd_norm_g': 1.0 + nrm(ks[24], (DEPTH, D_INNER), 0.02),
        'w_br_lru': nrm(ks[25], (DEPTH, LRU_WIDTH, D_MODEL), LRU_WIDTH ** -0.5),
        'w_br_ssd': nrm(ks[26], (DEPTH, D_INNER, D_MODEL), D_INNER ** -0.5),
        'w_out': nrm(ks[27], (DEPTH, D_MODEL, D_MODEL), D_MODEL ** -0.5),
        'norm_ffn2_g': 1.0 + nrm(ks[28], (DEPTH, D_MODEL), 0.02),
        'ffn2_w_up': nrm(ks[29], (DEPTH, D_MODEL, 2 * FFN_DIM), D_MODEL ** -0.5),
        'ffn2_w_down': nrm(ks[30], (DEPTH, FFN_DIM, D_MODEL), FFN_DIM ** -0.5),
        'norm_final_g': 1.0 + nrm(ks[31], (D_MODEL,), 0.02),
    }

def reference(x_prompt, x_sample, state_lru_conv, state_lru_h, state_ssd_conv, state_ssd_h,
              norm_ffn1_g, ffn1_w_up, ffn1_w_down, norm_mix_g, w_in, b_gate,
              lru_conv_w, lru_conv_b, lru_w_rg, lru_b_rg, lru_w_ig, lru_b_ig, lru_lambda,
              ssd_conv_w, ssd_conv_b, ssd_dt_bias, ssd_A_log, ssd_D, ssd_norm_g,
              w_br_lru, w_br_ssd, w_out, norm_ffn2_g, ffn2_w_up, ffn2_w_down, norm_final_g):
    nbp = x_prompt.shape[0]
    dtype = x_prompt.dtype
    xp, xs = x_prompt, x_sample
    new_p, new_s = [], []
    for l in range(DEPTH):
        p = {
            'norm_ffn1_g': norm_ffn1_g[l], 'ffn1_w_up': ffn1_w_up[l], 'ffn1_w_down': ffn1_w_down[l],
            'norm_mix_g': norm_mix_g[l], 'w_in': w_in[l], 'b_gate': b_gate[l],
            'lru_conv_w': lru_conv_w[l], 'lru_conv_b': lru_conv_b[l],
            'lru_w_rg': lru_w_rg[l], 'lru_b_rg': lru_b_rg[l],
            'lru_w_ig': lru_w_ig[l], 'lru_b_ig': lru_b_ig[l], 'lru_lambda': lru_lambda[l],
            'ssd_conv_w': ssd_conv_w[l], 'ssd_conv_b': ssd_conv_b[l],
            'ssd_dt_bias': ssd_dt_bias[l], 'ssd_A_log': ssd_A_log[l], 'ssd_D': ssd_D[l],
            'ssd_norm_g': ssd_norm_g[l], 'w_br_lru': w_br_lru[l], 'w_br_ssd': w_br_ssd[l],
            'w_out': w_out[l], 'norm_ffn2_g': norm_ffn2_g[l],
            'ffn2_w_up': ffn2_w_up[l], 'ffn2_w_down': ffn2_w_down[l],
        }
        xp, st_p = _layer(
            xp,
            jnp.zeros((nbp, CONV_W - 1, LRU_WIDTH), dtype),
            jnp.zeros((nbp, LRU_WIDTH), dtype),
            jnp.zeros((nbp, CONV_W - 1, SSD_CONV_DIM), dtype),
            jnp.zeros((nbp, SSD_HEADS, SSD_HEAD_DIM, D_STATE), dtype),
            p)
        xs, st_s = _layer(xs, state_lru_conv[l], state_lru_h[l], state_ssd_conv[l], state_ssd_h[l], p)
        new_p.append(st_p)
        new_s.append(st_s)
    y_prompt = _rmsnorm(xp, norm_final_g)
    y_sample = _rmsnorm(xs, norm_final_g)
    lru_conv_p = jnp.stack([s[0] for s in new_p])
    lru_h_p = jnp.stack([s[1] for s in new_p])
    ssd_conv_p = jnp.stack([s[2] for s in new_p])
    ssd_h_p = jnp.stack([s[3] for s in new_p])
    lru_conv_s = jnp.stack([s[0] for s in new_s])
    lru_h_s = jnp.stack([s[1] for s in new_s])
    ssd_conv_s = jnp.stack([s[2] for s in new_s])
    ssd_h_s = jnp.stack([s[3] for s in new_s])
    return (y_prompt, y_sample, lru_conv_p, lru_h_p, ssd_conv_p, ssd_h_p,
            lru_conv_s, lru_h_s, ssd_conv_s, ssd_h_s)


_drawn_inputs = setup_inputs


def setup_inputs(seed=0):
    import zlib

    import numpy as np

    out = dict(_drawn_inputs(seed))
    spreads = {}
    factors = {'norm_ffn1_g': 3.412,
     'b_gate': 8.0,
     'lru_b_rg': 24.261,
     'lru_b_ig': 8.0,
     'ssd_conv_b': 3.37,
     'ssd_D': 35.769,
     'ssd_norm_g': 20.053,
     'norm_ffn2_g': 7.829,
     'norm_final_g': 8.407}
    for name, (base, spread) in spreads.items():
        noise = np.random.default_rng([zlib.crc32(name.encode()), seed]).standard_normal(out[name].shape)
        drawn = base * np.exp(spread * noise) if base else spread * noise
        out[name] = jnp.asarray(drawn.astype(out[name].dtype))
    for name, factor in factors.items():
        out[name] = (out[name] * factor).astype(out[name].dtype)
    return out
```

```python
from contextlib import ExitStack

import concourse.bass as bass
from concourse import mybir

F32 = mybir.dt.float32
F32R = mybir.dt.float32r
ACT = mybir.ActivationFunctionType
ALU = mybir.AluOpType

P = 128
D_MODEL = 1024
SEQ, DEC_B, DEC_L = 512, 8, 16
TOK = SEQ + DEC_B * DEC_L
HALF = TOK // 2
KT = D_MODEL // P
NT = TOK // P
FFN = 2816
FFN_GROUPS = [8, 8, 6]
HEADS, HD, NS = 32, 64, 128
GROUPS, HPG = 4, 8
PAIRS = HPG // 2
D_INNER = 2048
CONV_TILES = KT + 24
COL_GATE, COL_Z, COL_XBC, COL_DT, COL_MIX = 1024, 2048, 4096, 7168, 7200
HIST = 3
EXT_P = HIST + SEQ
EXT = EXT_P + DEC_B * (HIST + DEC_L)
TAIL = HIST * (1 + DEC_B)
EPS = 1e-6
TINY = 1e-30
GELU_C, GELU_A = 0.7978845608028654, 0.044715

UP_UNITS = [2 * n for n in FFN_GROUPS]
FFN_UNITS = sum(UP_UNITS) + 8 * len(FFN_GROUPS)
PRE_OUTS = 2 + 2 * NT
U_FFN1, O_FFN1 = 0, PRE_OUTS
U_LRU, O_LRU = U_FFN1 + FFN_UNITS, O_FFN1 + FFN_UNITS
U_DT, O_DT = U_LRU + 2 * KT, O_LRU + 2 * KT
GRP_UNITS, GRP_OUTS = 18, 30
UG_Z, UG_MIX, UG_BR = 6, 10, 14
OG_Z = 6
OG_MIX = (10, 15, 20, 21)
OG_OLD, OG_NEW = (11, 16), (13, 18)
OG_BR = 22
U_GRP, O_GRP = U_DT + 1, O_DT + 1
U_MRG, O_MRG = U_GRP + GROUPS * GRP_UNITS, O_GRP + GROUPS * GRP_OUTS
U_OUT, O_OUT = U_MRG + KT, O_MRG + KT
O_TAIL = O_OUT + KT
TAIL_OUTS = 5
U_FFN2, O_FFN2 = U_OUT + KT, O_TAIL + TAIL_OUTS
U_END, O_FIN = U_FFN2 + FFN_UNITS, O_FFN2 + FFN_UNITS

V_SCW, V_SCB, V_LCB = 0, 96, 120
V_LCW, V_BR, V_BI, V_LAM, V_NF1, V_NMIX, V_NF2, V_SNG, V_BG = (128 + x for x in (0, 32, 40, 48, 56, 64, 72, 80, 96))
V_SET1 = 112

def norm_index(kind):
    return {"ffn1": 0, "mix": 1, "grp": 2, "ffn2": 2 + GROUPS}[kind]


SQ_FFN1, SQ_MIX, SQ_GRP, SQ_FFN2 = 0, KT, 2 * KT, 2 * KT + GROUPS * PAIRS

LV_P, LV_Q, LV_LA, LV_IX, LV_V, LV_U0, LV_AH, LV_U1, LV_A0, LV_SCAN, LV_Y = range(1, 12)
LV = 11
LA_G2, LA_TR, LA_TI, LA_TG, LA_A, LA_T2, LA_A2, LA_SQ = range(1, 9)
LA = 8
SA_BT, SA_L, SA_ES = 1, 2, 3
SA = 3
SV_CBM, SV_XD, SV_XDD, SV_G, SV_T1, SV_T2, SV_Y, SV_H0, SV_H1 = range(1, 10)
SV, SV_GRP = 9, 4 * 9 + 7
SP_XT, SP_CB, SP_SEG, SP_YD, SP_E, SP_YO, SP_ST = range(1, 8)
SP, SP_GRP = 7, 4 * 7 + 6


DT_V, DT_A = 16, 8
N_PARAMS, N_CONST = 17, 18


SEMAPHORES = """const xin0 xin1 xin2 xin3 xin4 params w_in0 w_in1 w_hi_done w_lo_done out_ready out_free
sq_done sq_summed rs_act rs_step xn_done xh_done xl_done ff_th ff_hi ff_lo start_v start_a
hist_in ext_in conv tail_in wg_in gates_mm lru_v lru_a htail_in spill e_out eg_in
dt_v dt_a dt_p gtr xb_th xb_out z_th z_out eq_mm eq_cp m_built ht_zero ssd_p ssd_a ssd_v bseq
h0_in hs_step hs_out hp_mm hp_cp hp_out yz acc_zero gate_th gate_out gate_in0 gate_in1 mg_b mg_v yl_hi_done yl_lo_done
mh_done ml_done reload tails_out gfin fin_a fin_v y_dma""".split()


def feature_tile(buf, i):
    return buf[:, bass.ds(i, 1), :].rearrange("p o n -> p (o n)")


def halves(ap):
    return ap.rearrange("p (h c) -> p h c", h=2)


def sampled(ap):
    return ap.rearrange("p (b c) -> p b c", b=DEC_B)


def layer(nc, x_prompt, x_sample, state_lru_conv, state_lru_h, state_ssd_conv, state_ssd_h,
          norm_ffn1_g, ffn1_w_up, ffn1_w_down, norm_mix_g, w_in, b_gate,
          lru_conv_w, lru_conv_b, lru_w_rg, lru_b_rg, lru_w_ig, lru_b_ig, lru_lambda,
          ssd_conv_w, ssd_conv_b, ssd_dt_bias, ssd_A_log, ssd_D, ssd_norm_g,
          w_br_lru, w_br_ssd, w_out, norm_ffn2_g, ffn2_w_up, ffn2_w_down, norm_final_g,
          y_prompt, y_sample, lru_conv_p, lru_h_p, ssd_conv_p, ssd_h_p,
          lru_conv_s, lru_h_s, ssd_conv_s, ssd_h_s):
    ctx = ExitStack()
    with ctx:
        def sb(stack, name, shape, dt=F32):
            return stack.enter_context(nc.sbuf_tensor(name, shape, dt))

        s = {n: ctx.enter_context(nc.semaphore(n)) for n in SEMAPHORES}

        resid = sb(ctx, "resid", [P, KT, TOK])
        act_hi = sb(ctx, "act_hi", [P, KT, TOK], F32R)
        act_lo = sb(ctx, "act_lo", [P, KT, TOK], F32R)
        w_raw = sb(ctx, "w_raw", [P, 2, KT, P])
        w_hi = sb(ctx, "w_hi", [P, 2, KT, P], F32R)
        w_lo = sb(ctx, "w_lo", [P, 2, KT, P], F32R)
        ident = sb(ctx, "ident", [P, P])
        ones = sb(ctx, "ones", [P, P])
        le_mask = sb(ctx, "le_mask", [P, 2, P])
        gt_mask = sb(ctx, "gt_mask", [P, 2, P])
        gt_r = sb(ctx, "gt_r", [P, 2, P], F32R)
        seq_mask = sb(ctx, "seq_mask", [P, DEC_B])
        sel = sb(ctx, "sel", [HPG, PAIRS, P])
        vec = sb(ctx, "vec", [P, 240])
        lru_c = sb(ctx, "lru_c", [P, KT])
        hist = sb(ctx, "hist", [P, CONV_TILES, DEC_B * HIST])
        tail = sb(ctx, "tail", [P, CONV_TILES, TAIL])
        h0_lru = sb(ctx, "h0_lru", [P, KT, DEC_B])
        h_tail = sb(ctx, "h_tail", [P, KT, 1 + DEC_B])
        head_vec = sb(ctx, "head_vec", [HEADS, 4])
        eps_col = sb(ctx, "eps_col", [P, 1])
        squares = sb(ctx, "squares", [P, 2, TOK])
        rstd = sb(ctx, "rstd", [P, TOK])
        rtmp = sb(ctx, "rtmp", [P, TOK])
        rvar = sb(ctx, "rvar", [P, TOK])

        with ExitStack() as sc:
            x_rows = sb(sc, "x_rows", [P, NT, D_MODEL])
            hist_rows = sb(sc, "hist_rows", [DEC_B * HIST, CONV_TILES * P])
            h0_rows = sb(sc, "h0_rows", [DEC_B, D_MODEL])
            vec_rows = sb(sc, "vec_rows", [P, 2, P])
            lam_t = sb(sc, "lam_t", [P, 8, KT])
        with ExitStack() as sc:
            h_hi = sb(sc, "h_hi", [P, 8, TOK], F32R)
            h_lo = sb(sc, "h_lo", [P, 8, TOK], F32R)
            ff_t = sb(sc, "ff_t", [P, TOK])
            ff_a = sb(sc, "ff_a", [P, TOK])
            ff_h = sb(sc, "ff_h", [P, TOK])
            tail_rows = sb(sc, "tail_rows", [TAIL, CONV_TILES * P])
            htail_rows = sb(sc, "htail_rows", [1 + DEC_B, D_MODEL])
            g_fin = sb(sc, "g_fin", [P, D_MODEL])
            y_out = sb(sc, "y_out", [P, 2, D_MODEL])
            fin = sb(sc, "fin", [P, 8, NT])
        y_sq = squares[:, :, 0:512]
        mix = ExitStack()
        acc_ssd = sb(mix, "acc_ssd", [P, KT, TOK])
        with ExitStack() as mrg:
            yl_hi = sb(mrg, "yl_hi", [P, KT, TOK], F32R)
            yl_lo = sb(mrg, "yl_lo", [P, KT, TOK], F32R)
            gates = sb(mrg, "gates", [P, 2, 2 * TOK])
            m_a, m_b = (sb(mrg, n, [P, TOK]) for n in ("m_a", "m_b"))
        with ExitStack() as ob:
            x_res = sb(ob, "x_res", [P, KT, TOK])
        ext = sb(mix, "ext", [P, EXT])
        with ExitStack() as sc:
            w_gates = sb(sc, "w_gates", [P, 2, P])
            xc, t_r, t_i, l_a, l_t2, l_a2, l_u, g_2, g_q, g_t, h_seq = (
                sb(sc, n, [P, TOK]) for n in
                ("xc", "t_r", "t_i", "l_a", "l_t2", "l_a2", "l_u", "g_2", "g_q", "g_t", "h_seq"))
            l_ah = sb(sc, "l_ah", [P, DEC_B])
        dt_col = sb(mix, "dt_col", [P, NT, HEADS])
        da_col = sb(mix, "da_col", [P, NT, HEADS])
        da_hr = sb(mix, "da_hr", [P, NT, HEADS], F32R)
        da_lo = sb(mix, "da_lo", [P, NT, HEADS])
        dd_col = sb(mix, "dd_col", [P, NT, HEADS])
        e_tot = sb(mix, "e_tot", [P, NT - 1, HEADS])
        with ExitStack() as sc:
            dt_x, dt_e, dt_w, dt_l, dt_row, da_row, keep, e_row = (
                sb(sc, n, [HEADS, TOK]) for n in
                ("dt_x", "dt_e", "dt_w", "dt_l", "dt_row", "da_row", "keep", "e_row"))
        e_g = sb(mix, "e_g", [HPG, TOK])
        d_g = sb(mix, "d_g", [HPG, 1])
        eq = sb(mix, "eq", [P, PAIRS * (DEC_B + 1)])
        xf = sb(mix, "xf", [P, PAIRS + 2, TOK])
        sz = sb(mix, "sz", [P, PAIRS, TOK])
        with ExitStack() as sc:
            m_hi = sb(sc, "m_hi", [P, HPG, P], F32R)
            m_lo = sb(sc, "m_lo", [P, HPG, P], F32R)
            lmat = sb(sc, "lmat", [P, HPG, P])
            cbm = sb(sc, "cbm", [P, P])
            b_tok = sb(sc, "b_tok", [P, P])
            xd = sb(sc, "xd", [P, HPG, HD])
            xdd = sb(sc, "xdd", [P, HPG, HD])
            ht = sb(sc, "ht", [P, HPG, HD])
            hp_rows = sb(sc, "hp_rows", [P, PAIRS, NS])
            b_seq = sb(sc, "b_seq", [P, DEC_B, NS])
            h0 = sb(sc, "h0", [P, 2, DEC_B, NS])
            h0_t = sb(sc, "h0_t", [P, 2, DEC_B, NS])
        es = rvar[:, 0:512]
        y_t = squares[:, 0, 0:512].rearrange("p (q l) -> p q l", q=PAIRS)
        with ExitStack() as sc:
            yn_hi = sb(sc, "yn_hi", [P, PAIRS, TOK], F32R)
            yn_lo = sb(sc, "yn_lo", [P, PAIRS, TOK], F32R)
        mix.close()

        pu = [ctx.enter_context(nc.psum_tensor(f"pu{i}", [P, 2, 512], F32)) for i in range(2)]
        pn = [ctx.enter_context(nc.psum_tensor(f"pn{i}", [P, 2, 512], F32)) for i in range(2)]

        x_spill = nc.dram_tensor("x_spill", [P, KT * TOK], F32, kind="Internal").ap()
        e_spill = nc.dram_tensor("e_spill", [HEADS, TOK], F32, kind="Internal").ap()

        gate_spill = nc.dram_tensor("gate_spill", [KT, P, 2 * TOK], F32, kind="Internal").ap()
        gate_buf = (rtmp[:, :], ext[:, HIST:HIST + TOK], ext[:, HIST:HIST + TOK], rtmp[:, :])

        def v(col, n=1):
            return vec[:, bass.ds(col, n)]

        def out(o):
            return pu[o % 2][:, :, 0:HALF]

        FFNS = ((U_FFN1, O_FFN1, 0, ffn1_w_up[0], ffn1_w_down[0]),
                (U_FFN2, O_FFN2, 22, ffn2_w_up[0], ffn2_w_down[0]))
        W_IN = w_in[0]
        h_src = state_ssd_h[0].rearrange("b (q two) p n -> q (two p) b n", two=2)
        h_dst = ssd_h_s[0].rearrange("b (q two) p n -> q (two p) b n", two=2)
        hp_dst = ssd_h_p[0, 0].rearrange("(q two) p n -> (two p) q n", two=2)

        def ffn_plan(u, o, ci):
            for gi, n in enumerate(FFN_GROUPS):
                yield gi, n, u, o, ci, u + 2 * n, o + 2 * n
                u, o, ci = u + 2 * n + KT, o + 2 * n + KT, ci + n

        block = ctx.enter_context(nc.Block())

        @block.sync
        def _(sp):
            def load(k, base, per, i, src, nk=KT, wide=False):
                side = (base + k) % 2
                if not (isinstance(i, int) and base + per * i + k < 2):
                    sp.wait_ge(s["w_lo_done"], per * i + (base + k - 1))
                dst = w_raw[:, side, 0:nk, :]
                if wide:
                    dst = w_raw[:, side, :, :].rearrange("p (k two) c -> p k (two c)", two=2)
                sp.dma_start(dst, src).then_inc(s[f"w_in{side}"], 16)

            def cols(w, c, k0=0, nk=KT, width=P):
                return w[k0 * P:(k0 + nk) * P, bass.ds(c, width)].rearrange("(k p) c -> p k c", p=P)

            def load_ffn(u, o, ci, w_up, w_down, first):
                tile0 = 0
                for gi, n, uu, _, _, ud, _ in ffn_plan(u, o, ci):
                    start = 0
                    if first and gi == 0:
                        for k in range(2):
                            load(k, 0, 2, 0, cols(w_up, k * FFN))
                        start = 1
                    with sp.Fori(start, n) as i:
                        for k in range(2):
                            load(k, uu, 2, i, cols(w_up, i * P + (tile0 * P + k * FFN)))
                    with sp.Fori(0, KT // 2) as i:
                        for k in range(2):
                            load(k, ud, 2, i, cols(w_down, i * (2 * P) + k * P, tile0, n), n)
                    tile0 += n

            for t in range(NT):
                src = x_prompt[0, t * P:(t + 1) * P, :] if t < NT - 1 else x_sample.rearrange("b l d -> (b l) d")
                sp.dma_start(x_rows[:, t, :], src).then_inc(s[f"xin{t}"], 16)
            load_ffn(*FFNS[0], True)
            with sp.Fori(0, KT) as j:
                for k in range(2):
                    load(k, U_LRU, 2, j, cols(W_IN, j * P + k * COL_GATE))
            load(0, U_DT, 1, 0, cols(W_IN, COL_DT))
            with sp.Fori(0, GROUPS) as g:
                for k in range(PAIRS):
                    load(k, U_GRP, GRP_UNITS, g, cols(W_IN, g * 512 + (COL_XBC + k * P)))
                for k in range(2):
                    load(4 + k, U_GRP, GRP_UNITS, g, cols(W_IN, g * P + (COL_XBC + D_INNER + k * 512)))
                for k in range(PAIRS):
                    load(UG_Z + k, U_GRP, GRP_UNITS, g, cols(W_IN, g * 512 + (COL_Z + k * P)))
                for f in range(4):
                    m, kind = divmod(f, 2)
                    load(UG_MIX + f, U_GRP, GRP_UNITS, g, cols(W_IN, g * 256 + (COL_MIX + kind * D_MODEL + m * P)))
                for r in range(4):
                    src = w_br_ssd[0][bass.ds(g * 512, 512), 256 * r:256 * (r + 1)].rearrange("(k p) c -> p k c", p=P)
                    load(UG_BR + r, U_GRP, GRP_UNITS, g, src, wide=True)
            sp.wait_ge(s["gate_out"], GROUPS * 64)
            with sp.Fori(1, KT // 2 + 1) as i1:
                for m in range(2):
                    load(m, U_MRG - 2, 2, i1, cols(w_br_lru[0], i1 * 256 + (m * P - 256)))
                for m in range(2):
                    sp.wait_ge(s["mg_v"], i1 * 2 + (m - 1))
                    sp.dma_start(gates[:, m, :], gate_spill[bass.ds(i1 * 2 + (m - 2), 1)].rearrange(
                        "o p t -> p (o t)")).then_inc(s[f"gate_in{m}"], 16)
            with sp.Fori(0, KT // 2) as i:
                for k in range(2):
                    load(k, U_OUT, 2, i, cols(w_out[0], i * 256 + k * P))
            load_ffn(*FFNS[1], False)
            for t in range(NT):
                sp.wait_ge(s["out_free"], O_FIN + t + 1)
                dst = y_prompt[0, t * P:(t + 1) * P, :] if t < NT - 1 else y_sample.rearrange("b l d -> (b l) d")
                sp.dma_start(dst, y_out[:, t % 2, :]).then_inc(s["y_dma"], 16)
                if t < NT - 1:
                    sp.wait_ge(s["y_dma"], 16 * (t + 1))
            sp.wait_ge(s["y_dma"], 16 * NT)

        @block.gpsimd
        def _(pool):
            steps = [0]

            def chain(ins):
                steps[0] += 1
                ins.then_inc(s["const"], 1)
                pool.wait_ge(s["const"], steps[0])

            chain(pool.memset(ident[:, :], 0.0))
            chain(pool.affine_select(out=ident[:, :], in_=ident[:, :], compare_op=ALU.not_equal, fill=1.0,
                                     base=0, pattern=[[-1, P]], channel_multiplier=1))
            chain(pool.memset(ones[:, :], 1.0))
            chain(pool.memset(le_mask[:, :, :], 1.0))
            chain(pool.memset(gt_mask[:, :, :], 1.0))
            chain(pool.memset(seq_mask[:, :], 1.0))
            chain(pool.memset(sel[:, :, :], 0.0))
            for m in range(2):
                chain(pool.affine_select(out=le_mask[:, m, :], in_=le_mask[:, m, :], compare_op=ALU.is_ge,
                                         fill=0.0, base=0, pattern=[[1, P]], channel_multiplier=-1))
                chain(pool.affine_select(out=gt_mask[:, m, :], in_=gt_mask[:, m, :], compare_op=ALU.is_ge,
                                         fill=0.0, base=-1, pattern=[[-1, P]], channel_multiplier=1))
            for mask, inner in ((sampled(le_mask[:, 1, :]), [[0, DEC_L]]), (sampled(gt_mask[:, 1, :]), [[0, DEC_L]]),
                                (seq_mask[:, :], [])):
                chain(pool.affine_select(out=mask, in_=mask, compare_op=ALU.is_ge, fill=0.0, base=0,
                                         pattern=[[-DEC_L, DEC_B]] + inner, channel_multiplier=1))
                chain(pool.affine_select(out=mask, in_=mask, compare_op=ALU.is_ge, fill=0.0, base=DEC_L - 1,
                                         pattern=[[DEC_L, DEC_B]] + inner, channel_multiplier=-1))
            v4 = sel[:, :, :].rearrange("h q (two p) -> h q two p", two=2)
            chain(pool.affine_select(out=v4, in_=v4, compare_op=ALU.not_equal, fill=1.0, base=0,
                                     pattern=[[-2, PAIRS], [-1, 2], [0, HD]], channel_multiplier=1))
            assert steps[0] == N_CONST, steps

            pool.wait_ge(s["out_free"], O_LRU)
            pool.dma_start(x_spill, resid[:, :, :].rearrange("p k t -> p (k t)")).then_inc(s["spill"], 16)
            pool.memset(ext[:, 0:HIST], 0.0).then_inc(s["hist_in"], 1)
            pool.memset(acc_ssd[:, 0, :], 0.0).then_inc(s["htail_in"], 1)
            pool.memset(acc_ssd[:, 1:KT, :], 0.0).then_inc(s["acc_zero"], 1)

            def history(n, c):
                pool.wait_ge(s["conv"], n * 7 + 1)
                dst = ext[:, EXT_P:EXT].rearrange("p (b c) -> p b c", b=DEC_B)[:, :, 0:HIST]
                src = hist[:, bass.ds(c, 1), :].rearrange("p o (b w) -> p (o b) w", b=DEC_B)
                pool.tensor_copy(dst, src).then_inc(s["hist_in"], 1)

            def last_rows(n, c):
                pool.wait_ge(s["ext_in"], n * 3 + 3)
                dst = tail[:, bass.ds(c, 1), :].rearrange("p o w -> p (o w)")
                pool.tensor_copy(dst[:, 0:HIST], ext[:, SEQ:EXT_P]).then_inc(s["tail_in"], 1)
                src = ext[:, EXT_P:EXT].rearrange("p (b c) -> p b c", b=DEC_B)[:, :, DEC_L:DEC_L + HIST]
                pool.tensor_copy(dst[:, HIST:TAIL].rearrange("p (b w) -> p b w", b=DEC_B), src).then_inc(s["tail_in"], 1)
                pool.wait_ge(s["tail_in"], n * 2 + 2)

            with pool.Fori(0, KT) as j:
                pool.wait_ge(s["gates_mm"], j + 1)
                pool.dma_start(w_gates[:, 0, :], lru_w_rg[0, bass.ds(j, 1)].rearrange("o i j -> i (o j)")).then_inc(s["wg_in"], 16)
                pool.dma_start(w_gates[:, 1, :], lru_w_ig[0, bass.ds(j, 1)].rearrange("o i j -> i (o j)")).then_inc(s["wg_in"], 16)
                history(j, j)
                last_rows(j, j)
                pool.wait_ge(s["lru_v"], j * LV + LV_SCAN)
                dst = h_tail[:, bass.ds(j, 1), :].rearrange("p o b -> p (o b)")
                pool.tensor_copy(dst[:, 0:1], h_seq[:, SEQ - 1:SEQ]).then_inc(s["htail_in"], 1)
                pool.tensor_copy(dst[:, 1:1 + DEC_B], h_seq[:, SEQ + DEC_L - 1:TOK:DEC_L]).then_inc(s["htail_in"], 1)

            pool.wait_ge(s["dt_v"], DT_V)
            pool.wait_ge(s["dt_a"], DT_A)
            pool.dma_start(e_spill, e_row[:, :]).then_inc(s["e_out"], 16)
            pool.wait_ge(s["e_out"], 16)
            with pool.Fori(0, GROUPS) as g:
                pool.wait_ge(s["out_free"], g * GRP_OUTS + O_GRP)
                pool.dma_start(e_g[:, :], e_spill[bass.ds(g * HPG, HPG), :]).then_inc(s["eg_in"], 16)
                with nc.allow_non_contiguous_dma(reason="one number per head"):
                    pool.dma_start(d_g[:, :], ssd_D[0, bass.ds(g * HPG, HPG)].rearrange("(h o) -> h o", o=1)).then_inc(s["eg_in"], 16)
                pool.memset(ht[:, :, :], 0.0).then_inc(s["ht_zero"], 1)

                def load_state(qq):
                    for a in range(2):
                        pool.dma_start(h0[:, a, :, :], h_src[bass.ds(g * PAIRS + (2 * qq + a), 1)].rearrange(
                            "o r b n -> r (o b) n")).then_inc(s["h0_in"], 16)

                load_state(0)
                for q in range(PAIRS + 2):
                    n = g * 6 + (KT + q)
                    c = g * PAIRS + (KT + q) if q < PAIRS else g + (KT + 16 + 4 * (q - PAIRS))
                    history(n, c)
                    last_rows(n, c)
                for t in range(NT):
                    if t > 0:
                        pool.wait_ge(s["ssd_p"], g * SP_GRP + (SP * (t - 1) + SP_SEG))
                    le = le_mask[:, t // (NT - 1), :].unsqueeze(1).to_broadcast([P, HPG, P])
                    for part, dst in ((da_hr, m_hi), (da_lo, m_lo)):
                        col = part[:, t, bass.ds(g * HPG, HPG)]
                        if part is da_hr:
                            col = col.bitcast(F32)
                        pool.tensor_tensor(dst[:, :, :], col.unsqueeze(2).to_broadcast([P, HPG, P]), le,
                                           ALU.mult).then_inc(s["m_built"], 1)
                pool.wait_ge(s["ssd_a"], g * (SA * NT) + (SA * (NT - 1) + SA_BT))
                pool.tensor_tensor(b_seq[:, :, :], b_tok[:, :].unsqueeze(1).to_broadcast([P, DEC_B, NS]),
                                   seq_mask[:, :].unsqueeze(2).to_broadcast([P, DEC_B, NS]),
                                   ALU.mult).then_inc(s["bseq"], 1)
                pool.wait_ge(s["hs_out"], g * 64 + 32)
                load_state(1)
                pool.wait_ge(s["hs_out"], g * 64 + 64)
                pool.wait_ge(s["hp_out"], g * 16 + 16)
                pool.wait_ge(s["gate_out"], g * 64 + 48)

            pool.wait_ge(s["out_free"], O_OUT)
            pool.dma_start(x_res[:, :, :].rearrange("p k t -> p (k t)"), x_spill).then_inc(s["reload"], 16)
            pool.wait_ge(s["out_free"], O_TAIL + TAIL_OUTS)
            pool.dma_start(lru_conv_p[0, 0], tail_rows[0:HIST, 0:D_MODEL]).then_inc(s["tails_out"], 16)
            pool.dma_start(ssd_conv_p[0, 0], tail_rows[0:HIST, D_MODEL:]).then_inc(s["tails_out"], 16)
            pool.dma_start(lru_conv_s[0].rearrange("b w c -> (b w) c"), tail_rows[HIST:TAIL, 0:D_MODEL]).then_inc(s["tails_out"], 16)
            pool.dma_start(ssd_conv_s[0].rearrange("b w c -> (b w) c"), tail_rows[HIST:TAIL, D_MODEL:]).then_inc(s["tails_out"], 16)
            pool.dma_start(lru_h_p[0], htail_rows[0:1, :]).then_inc(s["tails_out"], 16)
            pool.dma_start(lru_h_s[0], htail_rows[1:1 + DEC_B, :]).then_inc(s["tails_out"], 16)
            pool.dma_start(g_fin[:, :], norm_final_g.rearrange("(o d) -> o d", o=1).to_broadcast([P, D_MODEL])).then_inc(s["gfin"], 16)
            pool.wait_ge(s["tails_out"], 96)
            pool.wait_ge(s["gfin"], 16)

        @block.tensor
        def _(pe):
            def open_out(o):
                if not (isinstance(o, int) and o < 2):
                    pe.wait_ge(s["out_free"], o - 1)

            def products(dst, side, tiles, hi, lo, ready=None):
                n, at, ins = 3 * len(tiles), 0, None
                for k, c in tiles:
                    if ready:
                        ready(k)
                    for w, a in ((w_hi, hi), (w_hi, lo), (w_lo, hi)):
                        for h in range(2):
                            ins = pe.matmul(dst[:, h, :], w[:, side, c, :], a[:, k, h * HALF:(h + 1) * HALF],
                                            start=(at == 0), stop=(at == n - 1))
                        at += 1
                ins.then_inc(s["out_ready"], 1)

            def unit(ub, ob, per_u, per_o, i, hi, lo, nk=KT, ready=None):
                pe.wait_ge(s["w_lo_done"], i * per_u + (ub + 1))
                open_out(i * per_o + ob)
                products(out(ob), ub % 2, [(t, t) for t in range(nk)], hi, lo, ready)

            def norm_sum(sq0, count):
                for k in range(count):
                    pe.wait_ge(s["sq_done"], sq0 + (k + 1))
                    for h in range(2):
                        ins = pe.matmul(pn[0][:, h, 0:HALF], ones[:, :],
                                        squares[:, k % 2, h * HALF:(h + 1) * HALF],
                                        start=(k == 0), stop=(k == count - 1))
                    ins.then_inc(s["sq_summed"], 1)

            def ffn(u, o, ci, sq0):
                norm_sum(sq0, KT)

                def cut(k):
                    pe.wait_ge(s["xl_done"], sq0 + (k + 1))

                for gi, n, uu, ou, cc, ud, od in ffn_plan(u, o, ci):
                    with pe.Fori(0, n) as i:
                        for k in range(2):
                            unit(uu + k, ou + k, 2, 2, i, act_hi, act_lo,
                                 ready=cut if gi == 0 and k == 0 else None)

                    def hidden(k):
                        if k >= n - 2:
                            pe.wait_ge(s["ff_lo"], cc + (k + 1))

                    with pe.Fori(0, KT // 2) as i:
                        for k in range(2):
                            unit(ud + k, od + k, 2, 2, i, h_hi, h_lo, n, ready=hidden if k == 0 else None)

            pe.wait_ge(s["const"], N_CONST)
            for o in range(2 * NT):
                if o % 2 == 0:
                    pe.wait_ge(s[f"xin{o // 2}"], 16)
                open_out(o)
                for k in range(4):
                    ins = pe.transpose(pu[o % 2][:, 0, k * P:(k + 1) * P],
                                       x_rows[:, o // 2, (4 * (o % 2) + k) * P:(4 * (o % 2) + k + 1) * P], ident[:, :])
                ins.then_inc(s["out_ready"], 1)
            pe.wait_ge(s["params"], 16 * N_PARAMS)
            open_out(2 * NT)
            for c in range(CONV_TILES):
                ins = pe.transpose(pu[0][:, c // 16, (c % 16) * 24:(c % 16) * 24 + 24],
                                   hist_rows[:, c * P:(c + 1) * P], ident[0:24, 0:24])
            ins.then_inc(s["out_ready"], 1)
            open_out(2 * NT + 1)
            pe.transpose(pu[1][:, 0, 0:P], vec_rows[:, 0, :], ident[:, :]).then_inc(s["gates_mm"], 1)
            pe.transpose(pu[1][:, 0, P:P + V_SET1], vec_rows[0:V_SET1, 1, :], ident[0:V_SET1, 0:V_SET1])
            for c in range(KT):
                ins = pe.transpose(pu[1][:, 1, c * DEC_B:(c + 1) * DEC_B], h0_rows[:, c * P:(c + 1) * P],
                                   ident[0:DEC_B, 0:DEC_B])
            ins.then_inc(s["out_ready"], 1)

            ffn(U_FFN1, O_FFN1, 0, SQ_FFN1)

            norm_sum(SQ_MIX, KT)
            with pe.Fori(0, KT) as j:
                for k in range(2):
                    unit(U_LRU + k, O_LRU + k, 2, 2, j, act_hi, act_lo,
                         ready=(lambda t: pe.wait_ge(s["xl_done"], SQ_MIX + t + 1)) if k == 0 else None)
                pe.wait_ge(s["wg_in"], j * 32 + 32)
                pe.wait_ge(s["conv"], j * 7 + 8)
                for w in range(2):
                    for h in range(2):
                        ins = pe.matmul(pn[w][:, h, 0:HALF], w_gates[:, w, :], xc[:, h * HALF:(h + 1) * HALF],
                                        start=True, stop=True)
                ins.then_inc(s["gates_mm"], 1)

            unit(U_DT, O_DT, 1, 1, 0, act_hi, act_lo)
            pe.wait_ge(s["dt_v"], 12)
            for kind, row in enumerate((dt_row, da_row)):
                for t in range(NT):
                    c = (kind * NT + t) * HEADS
                    ins = pe.transpose(pn[0][:, 0, c:c + HEADS], row[:, t * P:(t + 1) * P], ident[0:HEADS, 0:HEADS])
            ins.then_inc(s["dt_p"], 1)
            pe.wait_ge(s["dt_v"], 14)
            for t in range(NT):
                pe.matmul(pn[1][:, 0, t * HEADS:(t + 1) * HEADS], gt_mask[:, t // (NT - 1), :], da_col[:, t, :],
                          start=True, stop=True)
            pe.matmul(pn[1][:, 1, 0:(NT - 1) * HEADS], ones[:, :],
                      da_col[:, 0:NT - 1, :].rearrange("p t h -> p (t h)"),
                      start=True, stop=True).then_inc(s["dt_p"], 1)
            pe.wait_ge(s["dt_a"], DT_A)

            with pe.Fori(0, GROUPS) as g:
                def grp_unit(k, nk=KT):
                    unit(U_GRP + k, O_GRP + k, GRP_UNITS, GRP_OUTS, g, act_hi, act_lo)

                def sv(t, step):
                    pe.wait_ge(s["ssd_v"], g * SV_GRP + (SV * t + step))

                def scores(t):
                    tile = slice(t * P, (t + 1) * P)
                    if t == 0:
                        pe.wait_ge(s["xb_out"], g * 6 + 6)
                    else:
                        sv(t - 1, SV_Y)
                    for q in range(PAIRS):
                        ins = pe.transpose(pn[0][:, 0, q * P:(q + 1) * P], xf[:, q, tile], ident[:, :])
                    ins.then_inc(s["ssd_p"], 1)
                    pe.transpose(pn[0][:, 1, 0:P], xf[:, PAIRS, tile], ident[:, :])
                    pe.matmul(pn[0][:, 1, P:2 * P], xf[:, PAIRS, tile], xf[:, PAIRS + 1, tile],
                              start=True, stop=True).then_inc(s["ssd_p"], 1)
                    pe.wait_ge(s["m_built"], g * (2 * NT) + (2 * t + 2))
                    if t == 0:
                        pe.wait_ge(s["eq_cp"], g + 1)
                    elif t < NT - 1:
                        sv(t - 1, SV_H1)
                    else:
                        pe.wait_ge(s["hp_cp"], g + 1)
                    for b in range(2):
                        for part, m in enumerate((m_hi, m_lo)):
                            ins = pe.matmul(pn[1][:, b, :], gt_r[:, t // (NT - 1), :],
                                            m[:, 4 * b:4 * b + 4, :].rearrange("p h l -> p (h l)"),
                                            start=(part == 0), stop=(part == 1))
                    ins.then_inc(s["ssd_p"], 1)

                def inner(t):
                    sv(t, SV_G)
                    for h in range(HPG):
                        r = HD * (h % 2)
                        ins = pe.matmul(pn[0][r:r + HD, 0, (h // 2) * P:(h // 2 + 1) * P], xd[:, h, :], lmat[:, h, :],
                                        start=True, stop=True)
                    ins.then_inc(s["ssd_p"], 1)
                    for q in range(PAIRS):
                        ins = pe.matmul(pn[1][:, 0, q * P:(q + 1) * P], sel[:, q, :], e_g[:, t * P:(t + 1) * P],
                                        start=True, stop=True)
                    ins.then_inc(s["ssd_p"], 1)

                def gate_unit(f):
                    unit(U_GRP + UG_MIX + f, O_GRP + OG_MIX[f], GRP_UNITS, GRP_OUTS, g, act_hi, act_lo)

                for k in range(PAIRS + 2):
                    grp_unit(k)
                pe.wait_ge(s["eg_in"], g * 32 + 32)
                for q in range(PAIRS):
                    c = q * (DEC_B + 1)
                    pe.matmul(pn[1][:, 0, c:c + DEC_B], sel[:, q, :], e_g[:, SEQ + DEC_L - 1:TOK:DEC_L],
                              start=True, stop=True)
                    ins = pe.matmul(pn[1][:, 0, c + DEC_B:c + DEC_B + 1], sel[:, q, :], d_g[:, :],
                                    start=True, stop=True)
                ins.then_inc(s["eq_mm"], 1)
                grp_unit(UG_Z)
                for t in range(NT - 1):
                    scores(t)
                    if t < NT - 2:
                        grp_unit(UG_Z + t + 1)
                    else:
                        gate_unit(0)
                    inner(t)
                    if t == 0:
                        pe.wait_ge(s["ht_zero"], g + 1)
                    for q in range(PAIRS):
                        ins = pe.matmul(pn[0][:, 1, q * P:(q + 1) * P],
                                        ht[:, 2 * q:2 * q + 2, :].rearrange("n a b -> n (a b)"),
                                        xf[:, PAIRS + 1, t * P:(t + 1) * P], start=True, stop=True)
                    ins.then_inc(s["ssd_p"], 1)
                    pe.matmul(pn[1][:, 1, :], b_tok[:, :], xdd[:, :, :].rearrange("p h d -> p (h d)"),
                              start=True, stop=True).then_inc(s["ssd_p"], 1)
                sv(NT - 2, SV_H1)
                for q in range(PAIRS):
                    ins = pe.transpose(pn[1][:, 1, q * P:(q + 1) * P],
                                       ht[:, 2 * q:2 * q + 2, :].rearrange("n a b -> n (a b)"), ident[:, :])
                ins.then_inc(s["hp_mm"], 1)
                scores(NT - 1)
                inner(NT - 1)
                pe.wait_ge(s["bseq"], g + 1)
                for qq in range(2):
                    pe.wait_ge(s["h0_in"], g * 64 + 32 * (qq + 1))
                    for a in range(2):
                        o = O_GRP + OG_OLD[qq] + a
                        open_out(g * GRP_OUTS + o)
                        for b in range(DEC_B):
                            ins = pe.transpose(pu[o % 2][:, b // 4, (b % 4) * P:(b % 4 + 1) * P], h0[:, a, b, :], ident[:, :])
                        ins.then_inc(s["out_ready"], 1)
                    for a in range(2):
                        q = 2 * qq + a
                        pe.wait_ge(s["out_free"], g * GRP_OUTS + (O_GRP + OG_OLD[qq] + a + 1))
                        for b in range(DEC_B):
                            c = SEQ + b * DEC_L
                            ins = pe.matmul(pn[0][:, 1, q * P + b * DEC_L:q * P + (b + 1) * DEC_L], h0_t[:, a, b, :],
                                            xf[:, PAIRS + 1, c:c + DEC_L], start=True, stop=True)
                    if qq == 1:
                        ins.then_inc(s["ssd_p"], 1)
                    for a in range(2):
                        o = O_GRP + OG_NEW[qq] + a
                        open_out(g * GRP_OUTS + o)
                        q = 2 * qq + a
                        for b in range(2):
                            ins = pe.matmul(pu[o % 2][:, b, :], xdd[:, 2 * q:2 * q + 2, :].rearrange("p h d -> p (h d)"),
                                            b_seq[:, 4 * b:4 * b + 4, :].rearrange("p b n -> p (b n)"),
                                            start=True, stop=True)
                        ins.then_inc(s["out_ready"], 1)
                    gate_unit(1 + qq)
                norm_sum(g * PAIRS + SQ_GRP, PAIRS)
                gate_unit(3)
                for r in range(4):
                    pe.wait_ge(s["w_lo_done"], g * GRP_UNITS + (U_GRP + UG_BR + r + 1))
                    for m in range(2):
                        o = O_GRP + OG_BR + 2 * r + m
                        open_out(g * GRP_OUTS + o)
                        products(out(o), (U_GRP + UG_BR + r) % 2, [(k, 2 * k + m) for k in range(PAIRS)], yn_hi, yn_lo,
                                 ready=(lambda k: pe.wait_ge(s["xl_done"], g * PAIRS + (SQ_GRP + k + 1)))
                                 if r == 0 and m == 0 else None)

            with pe.Fori(0, KT // 2) as i:
                for m in range(2):
                    unit(U_MRG + m, O_MRG + m, 2, 2, i, yl_hi, yl_lo,
                         ready=(lambda t: pe.wait_ge(s["yl_lo_done"], t + 1)) if m == 0 else None)
            with pe.Fori(0, KT // 2) as i:
                for k in range(2):
                    unit(U_OUT + k, O_OUT + k, 2, 2, i, act_hi, act_lo,
                         ready=(lambda t: pe.wait_ge(s["ml_done"], t + 1)) if k == 0 else None)
            for a in range(4):
                o = O_TAIL + a
                open_out(o)
                for b in range(8):
                    ins = pe.transpose(pu[o % 2][0:TAIL, b // 4, (b % 4) * P:(b % 4 + 1) * P], tail[:, 8 * a + b, :], ident[:, :])
                ins.then_inc(s["out_ready"], 1)
            o = O_TAIL + 4
            open_out(o)
            for b in range(KT):
                ins = pe.transpose(pu[o % 2][0:1 + DEC_B, b // 4, (b % 4) * P:(b % 4 + 1) * P], h_tail[:, b, :], ident[:, :])
            ins.then_inc(s["out_ready"], 1)

            ffn(U_FFN2, O_FFN2, 22, SQ_FFN2)

            pe.wait_ge(s["out_free"], O_FIN)
            for t in range(NT):
                o = O_FIN + t
                open_out(o)
                for k in range(KT):
                    ins = pe.transpose(pu[o % 2][:, k // 4, (k % 4) * P:(k % 4 + 1) * P], resid[:, k, t * P:(t + 1) * P], ident[:, :])
                ins.then_inc(s["out_ready"], 1)

        @block.scalar
        def _(act):
            def cut_weights(u, per, i):
                side = u % 2
                act.wait_ge(s[f"w_in{side}"], i * (8 * per) + 16 * (u // 2 + 1))
                act.activation(w_hi[:, side, :, :], w_raw[:, side, :, :], ACT.Copy).then_inc(s["w_hi_done"], 1)

            def take(u, o, per_u, per_o, i, ahead=True):
                act.wait_ge(s["out_ready"], i * per_o + (o + 1))
                if ahead:
                    cut_weights(u + 2, per_u, i)

            def norm(n, sq0, src, count, scale, ready):
                for k in range(count):
                    ready(k)
                    if k >= 2:
                        act.wait_ge(s["sq_summed"], sq0 + (k - 1))
                    act.activation(squares[:, k % 2, :], src[:, k, :], ACT.Square).then_inc(s["sq_done"], 1)
                act.wait_ge(s["sq_summed"], sq0 + count)
                act.activation(halves(rtmp[:, :]), pn[0][:, :, 0:HALF], ACT.Ln, scale=scale,
                               bias=eps_col[:, 0:1]).then_inc(s["rs_act"], 1)
                act.wait_ge(s["rs_act"], n * 2 + 1)
                act.activation(rstd[:, :], rtmp[:, :], ACT.Exp, scale=-0.5).then_inc(s["rs_act"], 1)

            def norm_cut(sq0, count, hi):
                for k in range(count):
                    act.wait_ge(s["xn_done"], sq0 + (k + 1))
                    act.activation(hi[:, k, :], squares[:, k % 2, :], ACT.Copy).then_inc(s["xh_done"], 1)

            def ffn(u, o, ci, n_norm, sq0, final):
                norm(n_norm, sq0, resid, KT, 1.0 / D_MODEL, lambda k: act.wait_ge(s["out_free"], o))
                norm_cut(sq0, KT, act_hi)
                for gi, n, uu, ou, cc, ud, od in ffn_plan(u, o, ci):
                    with act.Fori(0, n) as i:
                        take(uu, ou, 2, 2, i)
                        act.activation(halves(ff_t[:, :]), out(ou), ACT.Tanh, scale=0.5).then_inc(s["ff_th"], 1)
                        take(uu + 1, ou + 1, 2, 2, i)
                        act.wait_ge(s["out_free"], i * 2 + (ou + 2))
                        act.activation(feature_tile(h_hi, i), ff_h[:, :], ACT.Copy).then_inc(s["ff_hi"], 1)
                    last = final and gi == len(FFN_GROUPS) - 1
                    with act.Fori(0, KT // 2 - (1 if last else 0)) as i:
                        for k in range(2):
                            take(ud + k, od + k, 2, 2, i)

            rows = [(ssd_conv_w[0].rearrange("w (k p) -> (w k) p", p=P), 0, 0),
                    (ssd_conv_b[0].rearrange("(k p) -> k p", p=P), 0, V_SCB),
                    (lru_conv_b[0].rearrange("(k p) -> k p", p=P), 0, V_LCB),
                    (lru_conv_w[0].rearrange("w (k p) -> (w k) p", p=P), 1, V_LCW - 128)]
            for w, c in ((lru_b_rg, V_BR), (lru_b_ig, V_BI), (lru_lambda, V_LAM), (norm_ffn1_g, V_NF1),
                         (norm_mix_g, V_NMIX), (norm_ffn2_g, V_NF2), (ssd_norm_g, V_SNG), (b_gate, V_BG)):
                rows.append((w[0].rearrange("(k p) -> k p", p=P), 1, c - 128))
            for src, t, r in rows:
                act.dma_start(vec_rows[r:r + src.shape[0], t, :], src).then_inc(s["params"], 16)
            act.dma_start(hist_rows[:, 0:D_MODEL], state_lru_conv[0].rearrange("b w c -> (b w) c")).then_inc(s["params"], 16)
            act.dma_start(hist_rows[:, D_MODEL:], state_ssd_conv[0].rearrange("b w c -> (b w) c")).then_inc(s["params"], 16)
            act.dma_start(h0_rows[:, :], state_lru_h[0]).then_inc(s["params"], 16)
            with nc.allow_non_contiguous_dma(reason="one number per head"):
                act.dma_start(head_vec[:, 0:1], ssd_dt_bias[0].rearrange("(h o) -> h o", o=1)).then_inc(s["params"], 16)
                act.dma_start(head_vec[:, 1:2], ssd_A_log[0].rearrange("(h o) -> h o", o=1)).then_inc(s["params"], 16)
            assert len(rows) + 5 == N_PARAMS

            act.wait_ge(s["const"], N_CONST)
            cut_weights(0, 2, 0)
            cut_weights(1, 2, 0)
            lam = vec[:, V_LAM:V_LAM + KT]
            act.wait_ge(s["start_v"], 1)
            act.activation(lam_t[:, 0, :], lam, ACT.Abs).then_inc(s["start_a"], 1)
            act.wait_ge(s["start_a"], 1)
            act.activation(lam_t[:, 1, :], lam_t[:, 0, :], ACT.Exp, scale=-1.0).then_inc(s["start_a"], 1)
            act.wait_ge(s["start_v"], 2)
            act.activation(lam_t[:, 3, :], lam_t[:, 2, :], ACT.Ln).then_inc(s["start_a"], 1)

            ffn(U_FFN1, O_FFN1, 0, 0, SQ_FFN1, False)

            norm(1, SQ_MIX, resid, KT, 1.0 / D_MODEL, lambda k: act.wait_ge(s["out_free"], O_LRU))
            norm_cut(SQ_MIX, KT, act_hi)

            def to_ext(o, per_o, i, n):
                act.wait_ge(s["hist_in"], n + 2)
                act.activation(ext[:, HIST:HIST + HALF], pu[o % 2][:, 0, 0:HALF], ACT.Copy).then_inc(s["ext_in"], 1)
                act.activation(ext[:, HIST + HALF:EXT_P], pu[o % 2][:, 1, 0:SEQ - HALF], ACT.Copy).then_inc(s["ext_in"], 1)
                act.activation(ext[:, EXT_P:EXT].rearrange("p (b c) -> p b c", b=DEC_B)[:, :, HIST:],
                               sampled(pu[o % 2][:, 1, SEQ - HALF:HALF]), ACT.Copy).then_inc(s["ext_in"], 1)

            with act.Fori(0, KT) as j:
                def lv(step):
                    act.wait_ge(s["lru_v"], j * LV + step)

                def la(step):
                    act.wait_ge(s["lru_a"], j * LA + step)

                take(U_LRU, O_LRU, 2, 2, j)
                to_ext(O_LRU, 2, j, j)
                take(U_LRU + 1, O_LRU + 1, 2, 2, j)
                act.activation(halves(g_2[:, :]), out(O_LRU + 1), ACT.Square).then_inc(s["lru_a"], 1)
                act.wait_ge(s["gates_mm"], j + 2)
                act.activation(halves(t_r[:, :]), pn[0][:, :, 0:HALF], ACT.Tanh, scale=0.5,
                               bias=v(j + V_BR)).then_inc(s["lru_a"], 1)
                act.activation(halves(t_i[:, :]), pn[1][:, :, 0:HALF], ACT.Tanh, scale=0.5,
                               bias=v(j + V_BI)).then_inc(s["lru_a"], 1)
                lv(LV_Q)
                act.activation(g_t[:, :], g_q[:, :], ACT.Tanh, scale=GELU_C).then_inc(s["lru_a"], 1)
                lv(LV_LA)
                act.activation(l_a[:, :], t_r[:, :], ACT.Exp).then_inc(s["lru_a"], 1)
                act.activation(l_t2[:, :], t_r[:, :], ACT.Tanh).then_inc(s["lru_a"], 1)
                la(LA_A)
                act.activation(l_a2[:, :], l_a[:, :], ACT.Square).then_inc(s["lru_a"], 1)
                lv(LV_V)
                act.activation(l_u[:, :], l_t2[:, :], ACT.Sqrt, scale=-1.0).then_inc(s["lru_a"], 1)

            take(U_DT, O_DT, 1, 1, 0)
            act.wait_ge(s["out_free"], O_DT + 1)
            act.activation(dt_e[:, :], dt_x[:, :], ACT.Abs).then_inc(s["dt_a"], 1)
            act.wait_ge(s["dt_a"], 1)
            act.activation(dt_e[:, :], dt_e[:, :], ACT.Exp, scale=-1.0).then_inc(s["dt_a"], 1)
            act.activation(head_vec[:, 2:3], head_vec[:, 1:2], ACT.Exp).then_inc(s["dt_a"], 1)
            act.wait_ge(s["dt_v"], 1)
            act.activation(dt_l[:, :], dt_w[:, :], ACT.Ln).then_inc(s["dt_a"], 1)
            act.wait_ge(s["dt_v"], 12)
            act.activation(e_row[:, :], e_row[:, :], ACT.Exp).then_inc(s["dt_a"], 1)
            act.wait_ge(s["dt_v"], 14)
            act.activation(da_hr[:, :, :], da_col[:, :, :], ACT.Copy).then_inc(s["dt_a"], 1)
            act.wait_ge(s["dt_p"], 2)
            act.activation(dd_col[:, :, :].rearrange("p t h -> p (t h)"), pn[1][:, 0, 0:NT * HEADS], ACT.Exp).then_inc(s["dt_a"], 1)
            act.activation(e_tot[:, :, :].rearrange("p t h -> p (t h)"), pn[1][:, 1, 0:(NT - 1) * HEADS], ACT.Exp).then_inc(s["dt_a"], 1)

            with act.Fori(0, GROUPS) as g:
                def silu_z(q):
                    k = UG_Z + q
                    take(U_GRP + k, O_GRP + k, GRP_UNITS, GRP_OUTS, g)
                    act.wait_ge(s["out_free"], g * GRP_OUTS + (O_GRP + k))
                    act.activation(halves(rtmp[:, :]), out(O_GRP + k), ACT.Tanh, scale=0.5).then_inc(s["z_th"], 1)

                def gate(f):
                    m, kind = divmod(f, 2)
                    o = O_GRP + OG_MIX[f]
                    take(U_GRP + UG_MIX + f, o, GRP_UNITS, GRP_OUTS, g)
                    act.wait_ge(s["out_free"], g * GRP_OUTS + o)
                    if f > 0:
                        act.wait_ge(s["gate_out"], g * 64 + 16 * f)
                    act.activation(halves(gate_buf[f]), out(o), ACT.Tanh, scale=0.5,
                                   bias=v(g * 2 + (V_BG + kind * KT + m))).then_inc(s["gate_th"], 1)

                def gate_store(f):
                    m, kind = divmod(f, 2)
                    act.wait_ge(s["out_free"], g * GRP_OUTS + (O_GRP + OG_MIX[f] + 1))
                    act.dma_start(gate_spill[bass.ds(g * 2 + m, 1), :, kind * TOK:(kind + 1) * TOK].rearrange(
                        "o p t -> p (o t)"), gate_buf[f]).then_inc(s["gate_out"], 16)

                for k in range(PAIRS + 2):
                    take(U_GRP + k, O_GRP + k, GRP_UNITS, GRP_OUTS, g)
                    to_ext(O_GRP + k, GRP_OUTS, g, g * 6 + (KT + k))
                    act.wait_ge(s["conv"], g * 42 + (7 * (KT + k + 1) + 1))
                    act.activation(rtmp[:, :], xf[:, k, :], ACT.Tanh).then_inc(s["xb_th"], 1)
                act.wait_ge(s["xb_out"], g * 6 + 6)
                silu_z(0)
                for t in range(NT):
                    act.wait_ge(s["ssd_p"], g * SP_GRP + (SP * t + SP_CB))
                    act.activation(b_tok[:, :], pn[0][:, 1, 0:P], ACT.Copy).then_inc(s["ssd_a"], 1)
                    act.wait_ge(s["ssd_p"], g * SP_GRP + (SP * t + SP_SEG))
                    act.activation(lmat[:, :, :].rearrange("p (b h) l -> p b (h l)", b=2), pn[1][:, :, :],
                                   ACT.Exp).then_inc(s["ssd_a"], 1)
                    if t < NT - 2:
                        silu_z(t + 1)
                    elif t == NT - 2:
                        gate(0)
                    act.wait_ge(s["ssd_p"], g * SP_GRP + (SP * t + SP_E))
                    act.activation(es, pn[1][:, 0, :], ACT.Copy).then_inc(s["ssd_a"], 1)
                    if t == NT - 2:
                        gate_store(0)
                        act.wait_ge(s["hp_cp"], g + 1)
                        act.dma_start(hp_dst[:, bass.ds(g * PAIRS, PAIRS), :], hp_rows[:, :, :]).then_inc(s["hp_out"], 16)
                for qq in range(2):
                    for a in range(2):
                        act.wait_ge(s["out_free"], g * GRP_OUTS + (O_GRP + OG_NEW[qq] + a + 1))
                        act.dma_start(h_dst[bass.ds(g * PAIRS + (2 * qq + a), 1)].rearrange("o r b n -> r (o b) n"),
                                      h0[:, a, :, :]).then_inc(s["hs_out"], 16)
                    if qq == 0:
                        gate(1)
                        gate_store(1)

                def squared(k):
                    act.wait_ge(s["yz"], g * PAIRS + (k + 1))
                    if k == 2:
                        gate(2)
                        gate_store(2)

                norm(g + 2, g * PAIRS + SQ_GRP, xf, PAIRS, 0.25 / 512, squared)
                norm_cut(g * PAIRS + SQ_GRP, PAIRS, yn_hi)
                gate(3)
                gate_store(3)
                for r in range(4):
                    take(U_GRP + UG_BR + r, O_GRP + OG_BR + 2 * r + 1, GRP_UNITS, GRP_OUTS, g)
                act.wait_ge(s["gate_out"], g * 64 + 64)

            act.wait_ge(s["out_free"], O_MRG)
            for k in range(KT):
                act.activation(yl_hi[:, k, :], resid[:, k, :], ACT.Copy).then_inc(s["yl_hi_done"], 1)
            with act.Fori(0, KT // 2) as i:
                for m in range(2):
                    take(U_MRG + m, O_MRG + m, 2, 2, i)
            for k in range(KT):
                act.wait_ge(s["mg_v"], k + 3)
                act.activation(act_hi[:, k, :], resid[:, k, :], ACT.Copy).then_inc(s["mh_done"], 1)
            with act.Fori(0, KT // 2) as i:
                for k in range(2):
                    take(U_OUT + k, O_OUT + k, 2, 2, i)

            ffn(U_FFN2, O_FFN2, 22, 2 + GROUPS, SQ_FFN2, True)

            for t in range(NT):
                act.wait_ge(s["out_ready"], O_FIN + t + 1)
                if t:
                    act.wait_ge(s["fin_a"], 2 * t - 1)
                act.activation(y_sq, pu[(O_FIN + t) % 2][:, :, :], ACT.Square,
                               accum_out=fin[:, 0, t:t + 1]).then_inc(s["fin_a"], 1)
                act.wait_ge(s["fin_v"], 6 * t + 1)
                act.activation(fin[:, 2, t:t + 1], fin[:, 1, t:t + 1], ACT.Sqrt).then_inc(s["fin_a"], 1)

        @block.vector
        def _(dve):
            def stt(dst, a, scalar, b, op0, op1):
                return dve.scalar_tensor_tensor(out=dst, in0=a, scalar=scalar, in1=b, op0=op0, op1=op1)

            def cut_weights(u, per, i):
                side = u % 2
                dve.wait_ge(s["w_hi_done"], i * per + (u + 1))
                dve.tensor_tensor(w_lo[:, side, :, :], w_raw[:, side, :, :], w_hi[:, side, :, :].bitcast(F32),
                                  ALU.subtract).then_inc(s["w_lo_done"], 1)

            def take(u, o, per_u, per_o, i, ahead=True):
                if ahead:
                    cut_weights(u + 2, per_u, i)
                dve.wait_ge(s["out_ready"], i * per_o + (o + 1))

            def norm(n, sq0, src, count, scale, gain, hi, lo):
                dve.wait_ge(s["rs_act"], n * 2 + 2)
                var, r, t = rvar[:, :], rstd[:, :], rtmp[:, :]
                steps = [lambda: dve.tensor_scalar(halves(var), pn[0][:, :, 0:HALF], scale, EPS, ALU.mult, ALU.add),
                         lambda: dve.tensor_tensor(t, var, r, ALU.mult),
                         lambda: dve.tensor_tensor(t, t, r, ALU.mult),
                         lambda: dve.tensor_scalar(t, t, -0.5, 1.5, ALU.mult, ALU.add),
                         lambda: dve.tensor_tensor(r, r, t, ALU.mult)]
                for j, step in enumerate(steps):
                    step().then_inc(s["rs_step"], 1)
                    dve.wait_ge(s["rs_step"], n * 5 + (j + 1))

                def rest(k):
                    dve.wait_ge(s["xh_done"], sq0 + (k + 1))
                    dve.tensor_tensor(lo[:, k, :], squares[:, k % 2, :], hi[:, k, :].bitcast(F32),
                                      ALU.subtract).then_inc(s["xl_done"], 1)

                for k in range(count):
                    if k >= 2:
                        rest(k - 2)
                        dve.wait_ge(s["xl_done"], sq0 + (k - 1))
                    stt(squares[:, k % 2, :], src[:, k, :], v(gain(k)), r, ALU.mult, ALU.mult).then_inc(s["xn_done"], 1)
                for k in range(count - 2, count):
                    rest(k)

            def ffn(u, o, ci, n_norm, sq0, gain, final):
                norm(n_norm, sq0, resid, KT, 1.0 / D_MODEL, lambda k: gain + k, act_hi, act_lo)
                for gi, n, uu, ou, cc, ud, od in ffn_plan(u, o, ci):
                    with dve.Fori(0, n) as i:
                        take(uu, ou, 2, 2, i)
                        dve.wait_ge(s["ff_th"], i + (cc + 1))
                        stt(halves(ff_a[:, :]), halves(ff_t[:, :]), 1.0, out(ou), ALU.add, ALU.mult).then_inc(s["out_free"], 1)
                        take(uu + 1, ou + 1, 2, 2, i)
                        dve.wait_ge(s["out_free"], i * 2 + (ou + 1))
                        dve.tensor_tensor(halves(ff_h[:, :]), halves(ff_a[:, :]), out(ou + 1), ALU.mult).then_inc(s["out_free"], 1)
                        dve.wait_ge(s["ff_hi"], i + (cc + 1))
                        dve.tensor_tensor(feature_tile(h_lo, i), ff_h[:, :], feature_tile(h_hi, i).bitcast(F32),
                                          ALU.subtract).then_inc(s["ff_lo"], 1)
                    last = final and gi == len(FFN_GROUPS) - 1

                    def down(i, k, ahead=True):
                        take(ud + k, od + k, 2, 2, i, ahead)
                        r = halves(feature_tile(resid, i * 2 + k))
                        stt(r, out(od + k), 0.25, r, ALU.mult, ALU.add).then_inc(s["out_free"], 1)

                    with dve.Fori(0, KT // 2 - (1 if last else 0)) as i:
                        for k in range(2):
                            down(i, k)
                    if last:
                        for k in range(2):
                            down(KT // 2 - 1, k, False)

            def chained(name, base, ins, j):
                ins.then_inc(s[name], 1)
                dve.wait_ge(s[name], base + j)

            dve.memset(eps_col[:, :], EPS).then_inc(s["conv"], 1)
            for k in range(2):
                cut_weights(k, 2, 0)
            dve.wait_ge(s["const"], N_CONST)
            dve.tensor_copy(gt_r[:, :, :], gt_mask[:, :, :]).then_inc(s["gtr"], 1)
            for o in range(2 * NT):
                dve.wait_ge(s["out_ready"], o + 1)
                dve.tensor_copy(resid[:, 4 * (o % 2):4 * (o % 2) + 4, (o // 2) * P:(o // 2 + 1) * P],
                                pu[o % 2][:, 0, :].rearrange("p (k t) -> p k t", k=4)).then_inc(s["out_free"], 1)
            dve.wait_ge(s["out_ready"], 2 * NT + 1)
            dve.tensor_copy(hist[:, :, :].rearrange("p (b c) w -> p b (c w)", b=2), pu[0][:, :, 0:384]).then_inc(s["out_free"], 1)
            dve.wait_ge(s["out_ready"], 2 * NT + 2)
            chained("start_v", 0, dve.tensor_copy(vec[:, :], pu[1][:, 0, 0:240]), 1)
            dve.tensor_copy(h0_lru[:, :, :].rearrange("p k b -> p (k b)"), pu[1][:, 1, 0:KT * DEC_B]).then_inc(s["out_free"], 1)
            lt = [lam_t[:, k, :] for k in range(8)]
            lam = vec[:, V_LAM:V_LAM + KT]
            dve.wait_ge(s["start_a"], 2)
            chained("start_v", 0, dve.tensor_scalar(lt[2], lt[1], 1.0, None, ALU.add), 2)
            dve.wait_ge(s["start_a"], 3)
            chained("start_v", 0, dve.tensor_scalar(lt[4], lt[2], -1.0, TINY, ALU.add, ALU.add), 3)
            chained("start_v", 0, dve.reciprocal(lt[5], lt[4]), 4)
            chained("start_v", 0, stt(lt[6], lt[3], TINY, lt[1], ALU.add, ALU.mult), 5)
            chained("start_v", 0, dve.tensor_tensor(lt[6], lt[6], lt[5], ALU.mult), 6)
            chained("start_v", 0, dve.tensor_scalar(lt[7], lam, -1.0, 0.0, ALU.mult, ALU.max), 7)
            chained("start_v", 0, dve.tensor_tensor(lt[7], lt[7], lt[6], ALU.add), 8)
            chained("start_v", 0, dve.tensor_scalar(lru_c[:, :], lt[7], -4.0, None, ALU.mult), 9)
            for n, (a, b) in enumerate(((V_SCW, V_SCB + 24), (V_BR, V_BI + KT), (V_SNG, V_BG + 2 * KT))):
                chained("start_v", 0, dve.tensor_scalar(vec[:, a:b], vec[:, a:b], 0.5, None, ALU.mult), 10 + n)

            ffn(U_FFN1, O_FFN1, 0, 0, SQ_FFN1, V_NF1, False)

            norm(1, SQ_MIX, resid, KT, 1.0 / D_MODEL, lambda k: V_NMIX + k, act_hi, act_lo)
            dve.wait_ge(s["spill"], 16)

            def convolve(dst, n, per_o, i, o, w, step, bias):
                dve.wait_ge(s["ext_in"], n * 3 + 3)
                es_ = ext[:, EXT_P:EXT].rearrange("p (b c) -> p b c", b=DEC_B)
                dp, ds = dst[:, 0:SEQ], sampled(dst[:, SEQ:TOK])
                dve.tensor_scalar(dp, ext[:, 0:SEQ], v(w), v(bias), ALU.mult, ALU.add).then_inc(s["out_free"], 1)
                dve.tensor_scalar(ds, es_[:, :, 0:DEC_L], v(w), v(bias), ALU.mult, ALU.add).then_inc(s["conv"], 1)
                for k in range(1, 4):
                    if k == 1:
                        dve.wait_ge(s["out_free"], i * per_o + (o + 1))
                    else:
                        dve.wait_ge(s["conv"], n * 7 + (2 * k - 1))
                    stt(dp, ext[:, k:k + SEQ], v(w + step * k), dp, ALU.mult, ALU.add).then_inc(s["conv"], 1)
                    dve.wait_ge(s["conv"], n * 7 + 2 * k)
                    stt(ds, es_[:, :, k:k + DEC_L], v(w + step * k), ds, ALU.mult, ALU.add).then_inc(s["conv"], 1)

            with dve.Fori(0, KT) as j:
                def lv(step):
                    dve.wait_ge(s["lru_v"], j * LV + step)

                def la(step):
                    dve.wait_ge(s["lru_a"], j * LA + step)

                def done(ins):
                    ins.then_inc(s["lru_v"], 1)

                take(U_LRU, O_LRU, 2, 2, j)
                convolve(xc, j, 2, j, O_LRU, j + V_LCW, KT, j + V_LCB)
                take(U_LRU + 1, O_LRU + 1, 2, 2, j)
                la(LA_G2)
                done(dve.tensor_scalar(g_q[:, :], g_2[:, :], GELU_A, 1.0, ALU.mult, ALU.add))
                lv(LV_P)
                done(dve.tensor_tensor(halves(g_q[:, :]), halves(g_q[:, :]), out(O_LRU + 1), ALU.mult))
                la(LA_TI)
                done(dve.tensor_scalar(t_r[:, :], t_r[:, :], 1.0, lru_c[:, bass.ds(j, 1)], ALU.add, ALU.mult))
                done(stt(t_i[:, :], t_i[:, :], 1.0, xc[:, :], ALU.add, ALU.mult))
                la(LA_TG)
                stt(halves(g_t[:, :]), halves(g_t[:, :]), 1.0, out(O_LRU + 1), ALU.add, ALU.mult).then_inc(s["out_free"], 1)
                la(LA_A2)
                done(stt(l_t2[:, :], l_a2[:, :], 1.0, l_t2[:, :], ALU.add, ALU.mult))
                la(LA_SQ)
                done(stt(l_u[:, :], t_i[:, :], 0.5, l_u[:, :], ALU.mult, ALU.mult))
                a0, u0 = l_a[:, SEQ:TOK:DEC_L], l_u[:, SEQ:TOK:DEC_L]
                done(dve.tensor_tensor(l_ah[:, :], a0, h0_lru[:, bass.ds(j, 1), :].rearrange("p o b -> p (o b)"), ALU.mult))
                lv(LV_AH)
                done(dve.tensor_tensor(u0, u0, l_ah[:, :], ALU.add))
                done(dve.memset(a0, 0.0))
                lv(LV_A0)
                dve.wait_ge(s["htail_in"], j * 2 + 1)
                done(dve.tensor_tensor_scan(h_seq[:, :], l_a[:, :], l_u[:, :], 0.0, ALU.mult, ALU.add))
                lv(LV_SCAN)
                dve.wait_ge(s["out_free"], j * 2 + (O_LRU + 2))
                done(stt(feature_tile(resid, j), g_t[:, :], 0.5, h_seq[:, :], ALU.mult, ALU.mult))

            take(U_DT, O_DT, 1, 1, 0)
            dve.tensor_scalar(halves(dt_x[:, :]), out(O_DT)[0:HEADS], head_vec[:, 0:1], None, ALU.add).then_inc(s["out_free"], 1)
            dve.wait_ge(s["dt_a"], 3)
            chained("dt_v", 0, dve.tensor_scalar(dt_w[:, :], dt_e[:, :], 1.0, None, ALU.add), 1)
            dve.wait_ge(s["dt_a"], 4)
            chained("dt_v", 0, dve.tensor_scalar(dt_w[:, :], dt_w[:, :], -1.0, TINY, ALU.add, ALU.add), 2)
            chained("dt_v", 0, dve.reciprocal(dt_w[:, :], dt_w[:, :]), 3)
            chained("dt_v", 0, stt(dt_l[:, :], dt_l[:, :], TINY, dt_e[:, :], ALU.add, ALU.mult), 4)
            chained("dt_v", 0, dve.tensor_tensor(dt_l[:, :], dt_l[:, :], dt_w[:, :], ALU.mult), 5)
            chained("dt_v", 0, stt(dt_row[:, :], dt_x[:, :], 0.0, dt_l[:, :], ALU.max, ALU.add), 6)
            chained("dt_v", 0, dve.tensor_scalar(head_vec[:, 3:4], head_vec[:, 2:3], -1.0, None, ALU.mult), 7)
            chained("dt_v", 0, dve.tensor_scalar(da_row[:, :], dt_row[:, :], head_vec[:, 3:4], None, ALU.mult), 8)
            chained("dt_v", 0, dve.memset(keep[:, :], 1.0), 9)
            chained("dt_v", 0, dve.memset(keep[:, 0:SEQ:P], 0.0), 10)
            chained("dt_v", 0, dve.memset(keep[:, SEQ:TOK:DEC_L], 0.0), 11)
            chained("dt_v", 0, dve.tensor_tensor_scan(e_row[:, :], keep[:, :], da_row[:, :], 0.0, ALU.mult, ALU.add), 12)
            dve.wait_ge(s["dt_p"], 1)
            chained("dt_v", 0, dve.tensor_copy(dt_col[:, :, :].rearrange("p t h -> p (t h)"), pn[0][:, 0, 0:NT * HEADS]), 13)
            chained("dt_v", 0, dve.tensor_copy(da_col[:, :, :].rearrange("p t h -> p (t h)"), pn[0][:, 0, NT * HEADS:2 * NT * HEADS]), 14)
            dve.wait_ge(s["dt_a"], DT_A)
            chained("dt_v", 0, dve.tensor_tensor(da_lo[:, :, :], da_col[:, :, :], da_hr[:, :, :].bitcast(F32), ALU.subtract), 15)
            chained("dt_v", 0, dve.tensor_tensor(dd_col[:, :, :], dd_col[:, :, :], dt_col[:, :, :], ALU.mult), 16)

            with dve.Fori(0, GROUPS) as g:
                def done(ins):
                    ins.then_inc(s["ssd_v"], 1)

                def sp_(t, step):
                    dve.wait_ge(s["ssd_p"], g * SP_GRP + (SP * t + step))

                def sa(t, step):
                    dve.wait_ge(s["ssd_a"], g * (SA * NT) + (SA * t + step))

                def sv(t, step):
                    dve.wait_ge(s["ssd_v"], g * SV_GRP + (SV * t + step))

                def per_head(ap):
                    return ap.unsqueeze(2).to_broadcast([P, HPG, HD])

                def silu_z(q):
                    k = UG_Z + q
                    take(U_GRP + k, O_GRP + k, GRP_UNITS, GRP_OUTS, g)
                    dve.wait_ge(s["z_th"], g * PAIRS + (q + 1))
                    stt(halves(sz[:, q, :]), halves(rtmp[:, :]), 1.0, out(O_GRP + k), ALU.add, ALU.mult).then_inc(s["out_free"], 1)

                def gate(f):
                    take(U_GRP + UG_MIX + f, O_GRP + OG_MIX[f], GRP_UNITS, GRP_OUTS, g)
                    dve.wait_ge(s["gate_th"], g * 4 + (f + 1))
                    dve.tensor_scalar(gate_buf[f], gate_buf[f], 1.0, None, ALU.add).then_inc(s["out_free"], 1)

                for k in range(PAIRS + 2):
                    take(U_GRP + k, O_GRP + k, GRP_UNITS, GRP_OUTS, g)
                    c = g * PAIRS + k if k < PAIRS else g + (16 + 4 * (k - PAIRS))
                    convolve(xf[:, k, :], g * 6 + (KT + k), GRP_OUTS, g, O_GRP + k, c + V_SCW, 24, c + V_SCB)
                    dve.wait_ge(s["xb_th"], g * 6 + (k + 1))
                    stt(xf[:, k, :], rtmp[:, :], 1.0, xf[:, k, :], ALU.add, ALU.mult).then_inc(s["xb_out"], 1)
                dve.wait_ge(s["eq_mm"], g + 1)
                dve.tensor_copy(eq[:, :], pn[1][:, 0, 0:PAIRS * (DEC_B + 1)]).then_inc(s["eq_cp"], 1)
                silu_z(0)
                for t in range(NT):
                    tile = slice(t * P, (t + 1) * P)
                    sp_(t, SP_CB)
                    sa(t, SA_BT)
                    done(dve.tensor_tensor(cbm[:, :], pn[0][:, 1, P:2 * P], le_mask[:, t // (NT - 1), :], ALU.mult))
                    x_tok = pn[0][:, 0, :].rearrange("p (h d) -> p h d", h=HPG)
                    done(dve.tensor_tensor(xd[:, :, :], x_tok, per_head(dt_col[:, t, bass.ds(g * HPG, HPG)]), ALU.mult))
                    done(dve.tensor_tensor(xdd[:, :, :], x_tok, per_head(dd_col[:, t, bass.ds(g * HPG, HPG)]), ALU.mult))
                    sa(t, SA_L)
                    sv(t, SV_CBM)
                    done(dve.tensor_tensor(lmat[:, :, :], lmat[:, :, :], cbm[:, :].unsqueeze(1).to_broadcast([P, HPG, P]), ALU.mult))
                    if t < NT - 2:
                        silu_z(t + 1)
                    elif t == NT - 2:
                        gate(0)
                    else:
                        for qq in range(2):
                            for a in range(2):
                                o = O_GRP + OG_OLD[qq] + a
                                dve.wait_ge(s["out_ready"], g * GRP_OUTS + (o + 1))
                                dve.tensor_copy(h0_t[:, a, :, :].rearrange("p (c b) n -> p c (b n)", c=2),
                                                pu[o % 2][:, :, :]).then_inc(s["out_free"], 1)
                            for a in range(2):
                                q = 2 * qq + a
                                dec = eq[:, q * (DEC_B + 1):q * (DEC_B + 1) + DEC_B]
                                dve.tensor_tensor(h0[:, a, :, :], h0[:, a, :, :],
                                                  dec.unsqueeze(2).to_broadcast([P, DEC_B, NS]), ALU.mult).then_inc(s["hs_step"], 1)
                            for a in range(2):
                                o = O_GRP + OG_NEW[qq] + a
                                dve.wait_ge(s["out_ready"], g * GRP_OUTS + (o + 1))
                                dve.wait_ge(s["hs_step"], g * 4 + (2 * qq + a + 1))
                                hv = h0[:, a, :, :].rearrange("p (c b) n -> p c (b n)", c=2)
                                dve.tensor_tensor(hv, hv, pu[o % 2][:, :, :], ALU.add).then_inc(s["out_free"], 1)
                            if qq == 0:
                                gate(1)
                    sp_(t, SP_YO)
                    sa(t, SA_ES)
                    yv = y_t.rearrange("p q l -> p (q l)")
                    done(dve.tensor_tensor(yv, pn[0][:, 1, :], es, ALU.mult))
                    sv(t, SV_T1)
                    done(dve.tensor_tensor(yv, yv, pn[0][:, 0, :], ALU.add))
                    sv(t, SV_T2)
                    for q in range(PAIRS):
                        c = q * (DEC_B + 1) + DEC_B
                        ins = stt(xf[:, q, tile], xf[:, q, tile], eq[:, c:c + 1], y_t[:, q, :], ALU.mult, ALU.add)
                    done(ins)
                    if t < NT - 1:
                        done(dve.tensor_tensor(ht[:, :, :], ht[:, :, :], per_head(e_tot[:, t, bass.ds(g * HPG, HPG)]), ALU.mult))
                        sv(t, SV_H0)
                        sp_(t, SP_ST)
                        hv = ht[:, :, :].rearrange("p h d -> p (h d)")
                        done(dve.tensor_tensor(hv, hv, pn[1][:, 1, :], ALU.add))
                    if t == NT - 2:
                        dve.wait_ge(s["hp_mm"], g + 1)
                        dve.tensor_copy(hp_rows[:, :, :].rearrange("p q n -> p (q n)"), pn[1][:, 1, :]).then_inc(s["hp_cp"], 1)
                sv(NT - 1, SV_Y)
                for q in range(PAIRS):
                    dve.tensor_tensor(xf[:, q, :], xf[:, q, :], sz[:, q, :], ALU.mult).then_inc(s["yz"], 1)
                gate(2)
                norm(g + 2, g * PAIRS + SQ_GRP, xf, PAIRS, 0.25 / 512, lambda k: g * PAIRS + (V_SNG + k), yn_hi, yn_lo)
                gate(3)
                dve.wait_ge(s["acc_zero"], 1)
                for r in range(4):
                    for m in range(2):
                        o = O_GRP + OG_BR + 2 * r + m
                        if m == 1:
                            cut_weights(U_GRP + UG_BR + 2 + r, GRP_UNITS, g)
                        dve.wait_ge(s["out_ready"], g * GRP_OUTS + (o + 1))
                        acc = halves(acc_ssd[:, 2 * r + m, :])
                        dve.tensor_tensor(acc, acc, out(o), ALU.add).then_inc(s["out_free"], 1)

            for k in range(2):
                dve.memset(m_a[:, k:k + 1], 0.0).then_inc(s["mg_v"], 1)
            for k in range(KT):
                dve.wait_ge(s["yl_hi_done"], k + 1)
                dve.tensor_tensor(yl_lo[:, k, :], resid[:, k, :], yl_hi[:, k, :].bitcast(F32), ALU.subtract).then_inc(s["yl_lo_done"], 1)
            dve.wait_ge(s["yl_lo_done"], KT)
            with dve.Fori(0, KT // 2) as i:
                for m in range(2):
                    dve.wait_ge(s[f"gate_in{m}"], i * 16 + 16)
                    dve.wait_ge(s["mg_v"], i * 2 + (m + 2))
                    dve.tensor_tensor(m_b[:, :], gates[:, m, TOK:], feature_tile(acc_ssd, i * 2 + m), ALU.mult).then_inc(s["mg_b"], 1)
                    take(U_MRG + m, O_MRG + m, 2, 2, i)
                    dve.tensor_tensor(halves(m_a[:, :]), halves(gates[:, m, 0:TOK]), out(O_MRG + m), ALU.mult).then_inc(s["out_free"], 1)
                    dve.wait_ge(s["out_free"], i * 2 + (O_MRG + m + 1))
                    dve.wait_ge(s["mg_b"], i * 2 + (m + 1))
                    dve.tensor_tensor(feature_tile(resid, i * 2 + m), m_a[:, :], m_b[:, :], ALU.add).then_inc(s["mg_v"], 1)
            for k in range(KT):
                dve.wait_ge(s["mh_done"], k + 1)
                dve.tensor_tensor(act_lo[:, k, :], resid[:, k, :], act_hi[:, k, :].bitcast(F32), ALU.subtract).then_inc(s["ml_done"], 1)
            dve.wait_ge(s["reload"], 16)
            dve.wait_ge(s["ml_done"], KT)
            with dve.Fori(0, KT // 2) as i:
                for k in range(2):
                    take(U_OUT + k, O_OUT + k, 2, 2, i)
                    stt(halves(feature_tile(resid, i * 2 + k)), out(O_OUT + k), 0.5,
                        halves(feature_tile(x_res, i * 2 + k)), ALU.mult, ALU.add).then_inc(s["out_free"], 1)
            for a in range(5):
                o = O_TAIL + a
                dve.wait_ge(s["out_ready"], o + 1)
                dst, rows_ = (tail_rows[:, a * D_MODEL:(a + 1) * D_MODEL], TAIL) if a < 4 else (htail_rows[:, :], 1 + DEC_B)
                dve.tensor_copy(dst.rearrange("p (b c) -> p b c", b=2), pu[o % 2][0:rows_, :, :]).then_inc(s["out_free"], 1)

            ffn(U_FFN2, O_FFN2, 22, 2 + GROUPS, SQ_FFN2, V_NF2, True)

            dve.wait_ge(s["gfin"], 16)
            for t in range(NT):
                f = [fin[:, k, t:t + 1] for k in range(8)]
                dve.wait_ge(s["fin_a"], 2 * t + 1)
                chained("fin_v", 6 * t, dve.tensor_scalar(f[1], f[0], 1.0 / D_MODEL, EPS, ALU.mult, ALU.add), 1)
                dve.wait_ge(s["fin_a"], 2 * t + 2)
                chained("fin_v", 6 * t, dve.reciprocal(f[3], f[2]), 2)
                chained("fin_v", 6 * t, dve.tensor_tensor(f[4], f[1], f[3], ALU.mult), 3)
                chained("fin_v", 6 * t, dve.tensor_tensor(f[4], f[4], f[3], ALU.mult), 4)
                chained("fin_v", 6 * t, dve.tensor_scalar(f[4], f[4], -0.5, 1.5, ALU.mult, ALU.add), 5)
                chained("fin_v", 6 * t, dve.tensor_tensor(f[5], f[3], f[4], ALU.mult), 6)
                if t >= 2:
                    dve.wait_ge(s["y_dma"], 16 * (t - 1))
                stt(y_out[:, t % 2, :].rearrange("p (b c) -> p b c", b=2), pu[(O_FIN + t) % 2][:, :, :], f[5],
                    g_fin[:, :].rearrange("p (b c) -> p b c", b=2), ALU.mult, ALU.mult).then_inc(s["out_free"], 1)


_INS = ['x_prompt', 'x_sample', 'state_lru_conv', 'state_lru_h', 'state_ssd_conv', 'state_ssd_h',
        'norm_ffn1_g', 'ffn1_w_up', 'ffn1_w_down', 'norm_mix_g', 'w_in', 'b_gate',
        'lru_conv_w', 'lru_conv_b', 'lru_w_rg', 'lru_b_rg', 'lru_w_ig', 'lru_b_ig', 'lru_lambda',
        'ssd_conv_w', 'ssd_conv_b', 'ssd_dt_bias', 'ssd_A_log', 'ssd_D', 'ssd_norm_g',
        'w_br_lru', 'w_br_ssd', 'w_out', 'norm_ffn2_g', 'ffn2_w_up', 'ffn2_w_down', 'norm_final_g']
_OUTS = [(1, SEQ, D_MODEL), (DEC_B, DEC_L, D_MODEL),
         (1, 1, HIST, D_MODEL), (1, 1, D_MODEL), (1, 1, HIST, 24 * P), (1, 1, HEADS, HD, NS),
         (1, DEC_B, HIST, D_MODEL), (1, DEC_B, D_MODEL), (1, DEC_B, HIST, 24 * P), (1, DEC_B, HEADS, HD, NS)]


def kernel(**inputs):
    import numpy as _np
    import concourse.bacc as _bacc
    from concourse import mybir as _mybir
    from concourse.bass_utils import run_bass_kernel_spmd as _run

    nc = _bacc.Bacc("TRN2", target_bir_lowering=False, num_devices=1)
    arrays, args = {}, []
    for name in _INS:
        a = _np.ascontiguousarray(inputs[name])
        arrays[f"in_{name}_dram"] = a
        args.append(nc.dram_tensor(f"in_{name}_dram", a.shape, _mybir.dt.from_np(a.dtype), kind="ExternalInput").ap())
    for i, shape in enumerate(_OUTS):
        args.append(nc.dram_tensor(f"out_{i}_dram", shape, _mybir.dt.float32, kind="ExternalOutput").ap())
    layer(nc, *args)
    r = _run(nc, [arrays], core_ids=[0])
    return tuple(r.results[0][f"out_{i}_dram"] for i in range(len(_OUTS)))
```

```python
from contextlib import ExitStack

import concourse.bass as bass
from concourse import mybir

F32 = mybir.dt.float32
F32R = mybir.dt.float32r
ACT = mybir.ActivationFunctionType
ALU = mybir.AluOpType

P = 128
D_MODEL = 1024
SEQ, DEC_B, DEC_L = 512, 8, 16
TOK = SEQ + DEC_B * DEC_L
HALF = TOK // 2
KT = D_MODEL // P
NT = TOK // P
FFN = 2816
FFN_GROUPS = [8, 8, 6]
HEADS, HD, NS = 32, 64, 128
GROUPS, HPG = 4, 8
PAIRS = HPG // 2
D_INNER = 2048
CONV_TILES = KT + 24
COL_GATE, COL_Z, COL_XBC, COL_DT, COL_MIX = 1024, 2048, 4096, 7168, 7200
HIST = 3
EXT_P = HIST + SEQ
EXT = EXT_P + DEC_B * (HIST + DEC_L)
TAIL = HIST * (1 + DEC_B)
EPS = 1e-6
TINY = 1e-30
GELU_C, GELU_A = 0.7978845608028654, 0.044715

UP_UNITS = [2 * n for n in FFN_GROUPS]
FFN_UNITS = sum(UP_UNITS) + 8 * len(FFN_GROUPS)
PRE_OUTS = 2 + 2 * NT
U_FFN1, O_FFN1 = 0, PRE_OUTS
U_LRU, O_LRU = U_FFN1 + FFN_UNITS, O_FFN1 + FFN_UNITS
U_DT, O_DT = U_LRU + 2 * KT - 1, O_LRU + 2 * KT - 1
GRP_UNITS, GRP_OUTS = 18, 30
UG_Z, UG_MIX, UG_BR = 6, 10, 14
OG_Z = 6
OG_MIX = (10, 13, 20, 21)
OG_OLD, OG_NEW = (11, 14), (16, 18)
OG_BR = 22
U_GRP, O_GRP = U_DT + 2, O_DT + 2
U_MRG, O_MRG = U_GRP + GROUPS * GRP_UNITS, O_GRP + GROUPS * GRP_OUTS
O_TAIL, TAIL_OUTS = O_MRG + KT, 5
U_OUT, O_OUT = U_MRG + KT, O_TAIL + TAIL_OUTS
U_FFN2, O_FFN2 = U_OUT + KT, O_OUT + KT
U_END, O_FIN = U_FFN2 + FFN_UNITS, O_FFN2 + FFN_UNITS

V_SCW, V_SCB, V_LCB = 0, 96, 120
V_LCW, V_BR, V_BI, V_LAM, V_NF1, V_NMIX, V_NF2, V_SNG, V_BG = (128 + x for x in (0, 32, 40, 48, 56, 64, 72, 80, 96))
V_SET1 = 112

SQG = PAIRS + 1
SQ_FFN1, SQ_MIX, SQ_GRP, SQ_FFN2 = 0, KT, 2 * KT, 2 * KT + GROUPS * SQG
XN_FFN1, XN_MIX, XN_GRP, XN_FFN2 = 0, KT, 2 * KT, 2 * KT + GROUPS * PAIRS

LV_P, LV_Q, LV_LA, LV_IX, LV_V, LV_U0, LV_AH, LV_U1, LV_A0, LV_SCAN, LV_Y = range(1, 12)
LV = 11
LA_G2, LA_TR, LA_TI, LA_TG, LA_A, LA_T2, LA_A2, LA_SQ = range(1, 9)
LA = 8
SA_BT, SA_L, SA_ES = 1, 2, 3
SA = 3
SV_CBM, SV_XD, SV_XDD, SV_G, SV_T1, SV_T2, SV_H0, SV_H1, SV_Y = range(1, 10)
SV, SV_Y_LAST = 9, 7
SV_GRP = 4 * SV + SV_Y_LAST
SP_XT, SP_CB, SP_SEG, SP_YD, SP_E, SP_YO, SP_ST = range(1, 8)
SP, SP_GRP = 7, 4 * 7 + 6


DT_V, DT_A = 16, 8
N_PARAMS, N_CONST = 17, 18


SEMAPHORES = """const xin0 xin1 xin2 xin3 xin4 params w_in0 w_in1 w_hi_done w_lo_done out_ready out_free
sq_clear sq_done sq_part sq_added sq_summed ln_ready rs_act rs_step xn_done xh_done xl_done ff_th ff_hi ff_lo start_v start_a
hist_in ext_in conv tail_in wg_in gates_mm lru_v lru_a htail_in spill e_out eg_in
dt_v dt_a dt_p gtr xb_th xb_out z_th eq_mm eq_cp m_built ht_zero ssd_p ssd_a ssd_v bseq
h0_in0 h0_in1 hs_step hs_out hp_mm hp_cp hp_out yz acc_zero gate_th gate_out gate_in0 gate_in1 mg_b mg_v yl_hi_done yl_lo_done
mh_done ml_done reload tails_out gfin fin_a fin_v y_dma""".split()


def feature_tile(buf, i):
    return buf[:, bass.ds(i, 1), :].rearrange("p o n -> p (o n)")


def halves(ap):
    return ap.rearrange("p (h c) -> p h c", h=2)


def sampled(ap):
    return ap.rearrange("p (b c) -> p b c", b=DEC_B)


def layer(nc, x_prompt, x_sample, state_lru_conv, state_lru_h, state_ssd_conv, state_ssd_h,
          norm_ffn1_g, ffn1_w_up, ffn1_w_down, norm_mix_g, w_in, b_gate,
          lru_conv_w, lru_conv_b, lru_w_rg, lru_b_rg, lru_w_ig, lru_b_ig, lru_lambda,
          ssd_conv_w, ssd_conv_b, ssd_dt_bias, ssd_A_log, ssd_D, ssd_norm_g,
          w_br_lru, w_br_ssd, w_out, norm_ffn2_g, ffn2_w_up, ffn2_w_down, norm_final_g,
          y_prompt, y_sample, lru_conv_p, lru_h_p, ssd_conv_p, ssd_h_p,
          lru_conv_s, lru_h_s, ssd_conv_s, ssd_h_s):
    ctx = ExitStack()
    with ctx:
        def sb(stack, name, shape, dt=F32):
            return stack.enter_context(nc.sbuf_tensor(name, shape, dt))

        s = {n: ctx.enter_context(nc.semaphore(n)) for n in SEMAPHORES}

        resid = sb(ctx, "resid", [P, KT, TOK])
        act_hi = sb(ctx, "act_hi", [P, KT, TOK], F32R)
        act_lo = sb(ctx, "act_lo", [P, KT, TOK], F32R)
        w_raw = sb(ctx, "w_raw", [P, 2, KT, P])
        w_hi = sb(ctx, "w_hi", [P, 2, KT, P], F32R)
        w_lo = sb(ctx, "w_lo", [P, 2, KT, P], F32R)
        ident = sb(ctx, "ident", [P, P])
        ones = sb(ctx, "ones", [P, P])
        le_mask = sb(ctx, "le_mask", [P, 2, P])
        gt_mask = sb(ctx, "gt_mask", [P, 2, P])
        gt_r = sb(ctx, "gt_r", [P, 2, P], F32R)
        seq_mask = sb(ctx, "seq_mask", [P, DEC_B])
        sel = sb(ctx, "sel", [HPG, PAIRS, P])
        vec = sb(ctx, "vec", [P, 240])
        lam_t = sb(ctx, "lam_t", [P, 8, KT])
        lru_c = sb(ctx, "lru_c", [P, KT])
        tail = sb(ctx, "tail", [P, CONV_TILES, TAIL])
        h0_lru = sb(ctx, "h0_lru", [P, KT, DEC_B])
        h_tail = sb(ctx, "h_tail", [P, KT, 1 + DEC_B])
        head_vec = sb(ctx, "head_vec", [HEADS, 4])
        eps_col = sb(ctx, "eps_col", [P, 1])
        ln_col = sb(ctx, "ln_col", [P, 1])
        squares = sb(ctx, "squares", [P, 2, TOK])
        rstd = sb(ctx, "rstd", [P, TOK])
        rtmp = sb(ctx, "rtmp", [P, TOK])
        rvar = sb(ctx, "rvar", [P, TOK])

        with ExitStack() as sc:
            x_rows = sb(sc, "x_rows", [P, NT, D_MODEL])
            hist_rows = sb(sc, "hist_rows", [DEC_B * HIST, CONV_TILES * P])
            h0_rows = sb(sc, "h0_rows", [DEC_B, D_MODEL])
            vec_rows = sb(sc, "vec_rows", [P, 2, P])
        with ExitStack() as sc:
            h_hi = sb(sc, "h_hi", [P, 8, TOK], F32R)
            h_lo = sb(sc, "h_lo", [P, 8, TOK], F32R)
            ff_t = sb(sc, "ff_t", [P, TOK])
            ff_a = sb(sc, "ff_a", [P, TOK])
            ff_h = sb(sc, "ff_h", [P, TOK])
            tail_rows = sb(sc, "tail_rows", [TAIL, CONV_TILES * P])
            htail_rows = sb(sc, "htail_rows", [1 + DEC_B, D_MODEL])
            g_fin = sb(sc, "g_fin", [P, D_MODEL])
            y_out = sb(sc, "y_out", [P, 2, D_MODEL])
            fin = sb(sc, "fin", [P, 8, NT])
        y_sq = squares[:, :, 0:512]
        mix = ExitStack()
        acc_ssd = sb(mix, "acc_ssd", [P, KT, TOK])
        with ExitStack() as mrg:
            yl_hi = sb(mrg, "yl_hi", [P, KT, TOK], F32R)
            yl_lo = sb(mrg, "yl_lo", [P, KT, TOK], F32R)
            gates = sb(mrg, "gates", [P, 2, 2 * TOK])
            m_a, m_b = (sb(mrg, n, [P, TOK]) for n in ("m_a", "m_b"))
        with ExitStack() as ob:
            x_res = sb(ob, "x_res", [P, KT, TOK])
        ext = sb(mix, "ext", [P, EXT])
        dt_col = sb(mix, "dt_col", [P, NT, HEADS])
        da_col = sb(mix, "da_col", [P, NT, HEADS])
        da_hr = sb(mix, "da_hr", [P, NT, HEADS], F32R)
        da_lo = sb(mix, "da_lo", [P, NT, HEADS])
        dd_col = sb(mix, "dd_col", [P, NT, HEADS])
        e_tot = sb(mix, "e_tot", [P, NT - 1, HEADS])
        with ExitStack() as sc:
            dt_x, dt_e, dt_w, dt_l, dt_row, da_row, keep, e_row = (
                sb(sc, n, [HEADS, TOK]) for n in
                ("dt_x", "dt_e", "dt_w", "dt_l", "dt_row", "da_row", "keep", "e_row"))
            with ExitStack() as lru:
                w_gates = sb(lru, "w_gates", [P, 2, P])
                xc, t_r, t_i, l_a, l_t2, l_a2, l_u, g_2, g_q, g_t, h_seq = (
                    sb(lru, n, [P, TOK]) for n in
                    ("xc", "t_r", "t_i", "l_a", "l_t2", "l_a2", "l_u", "g_2", "g_q", "g_t", "h_seq"))
                l_ah = sb(lru, "l_ah", [P, DEC_B])
        e_g = sb(mix, "e_g", [HPG, TOK])
        d_g = sb(mix, "d_g", [HPG, 1])
        eq = sb(mix, "eq", [P, PAIRS * (DEC_B + 1)])
        xf = sb(mix, "xf", [P, PAIRS + 2, TOK])
        sz = sb(mix, "sz", [P, PAIRS, TOK])
        with ExitStack() as sc:
            lmat = sb(sc, "lmat", [P, HPG, P])
            cbm = sb(sc, "cbm", [P, P])
            b_tok = sb(sc, "b_tok", [P, P])
            xd = sb(sc, "xd", [P, HPG, HD])
            xdd = sb(sc, "xdd", [P, HPG, HD])
            ht = sb(sc, "ht", [P, HPG, HD])
            b_seq = sb(sc, "b_seq", [P, DEC_B, NS])
            h0_t = sb(sc, "h0_t", [P, 2, DEC_B, NS])
            es = sb(sc, "es", [P, PAIRS * P])
            y_t = sb(sc, "y_t", [P, PAIRS, P])
            hp_rows = sb(sc, "hp_rows", [P, PAIRS, NS])
            h0_a = sb(sc, "h0_a", [P, 2, DEC_B, NS])
            with ExitStack() as dc:
                m_hi = sb(dc, "m_hi", [P, HPG, P], F32R)
                m_lo = sb(dc, "m_lo", [P, HPG, P], F32R)
            h0_b = sb(sc, "h0_b", [P, 2, DEC_B, NS])
        h0 = (h0_a, h0_b)
        with ExitStack() as sc:
            yn_hi = sb(sc, "yn_hi", [P, PAIRS, TOK], F32R)
            yn_lo = sb(sc, "yn_lo", [P, PAIRS, TOK], F32R)
        mix.close()

        pu = [ctx.enter_context(nc.psum_tensor(f"pu{i}", [P, 2, 512], F32)) for i in range(2)]
        pn = [ctx.enter_context(nc.psum_tensor(f"pn{i}", [P, 2, 512], F32)) for i in range(2)]

        x_spill = nc.dram_tensor("x_spill", [P, KT * TOK], F32, kind="Internal").ap()
        e_spill = nc.dram_tensor("e_spill", [HEADS, TOK], F32, kind="Internal").ap()

        gate_spill = nc.dram_tensor("gate_spill", [KT, P, 2 * TOK], F32, kind="Internal").ap()
        gate_buf = (rtmp[:, :], ext[:, HIST:HIST + TOK], ext[:, HIST:HIST + TOK], rtmp[:, :])

        def v(col, n=1):
            return vec[:, bass.ds(col, n)]

        def out(o):
            return pu[o % 2][:, :, 0:HALF]

        FFNS = ((U_FFN1, O_FFN1, 0, ffn1_w_up[0], ffn1_w_down[0]),
                (U_FFN2, O_FFN2, 22, ffn2_w_up[0], ffn2_w_down[0]))
        W_IN = w_in[0]
        h_src = state_ssd_h[0].rearrange("b (q two) p n -> q (two p) b n", two=2)
        h_dst = ssd_h_s[0].rearrange("b (q two) p n -> q (two p) b n", two=2)
        hp_dst = ssd_h_p[0, 0].rearrange("(q two) p n -> (two p) q n", two=2)

        def ffn_plan(u, o, ci):
            for gi, n in enumerate(FFN_GROUPS):
                yield gi, n, u, o, ci, u + 2 * n, o + 2 * n
                u, o, ci = u + 2 * n + KT, o + 2 * n + KT, ci + n

        block = ctx.enter_context(nc.Block())

        @block.sync
        def _(sp):
            def load(k, base, per, i, src, nk=KT, wide=False):
                side = (base + k) % 2
                if not (isinstance(i, int) and base + per * i + k < 2):
                    sp.wait_ge(s["w_lo_done"], per * i + (base + k - 1))
                dst = w_raw[:, side, 0:nk, :]
                if wide:
                    dst = w_raw[:, side, :, :].rearrange("p (k two) c -> p k (two c)", two=2)
                sp.dma_start(dst, src).then_inc(s[f"w_in{side}"], 16)

            def cols(w, c, k0=0, nk=KT, width=P):
                return w[k0 * P:(k0 + nk) * P, bass.ds(c, width)].rearrange("(k p) c -> p k c", p=P)

            def load_ffn(u, o, ci, w_up, w_down, first):
                tile0 = 0
                for gi, n, uu, _, _, ud, _ in ffn_plan(u, o, ci):
                    start = 0
                    if first and gi == 0:
                        for k in range(2):
                            load(k, 0, 2, 0, cols(w_up, k * FFN))
                        start = 1
                    with sp.Fori(start, n) as i:
                        for k in range(2):
                            load(k, uu, 2, i, cols(w_up, i * P + (tile0 * P + k * FFN)))
                    with sp.Fori(0, KT // 2) as i:
                        for k in range(2):
                            load(k, ud, 2, i, cols(w_down, i * (2 * P) + k * P, tile0, n), n)
                    tile0 += n

            for t in range(NT):
                src = x_prompt[0, t * P:(t + 1) * P, :] if t < NT - 1 else x_sample.rearrange("b l d -> (b l) d")
                sp.dma_start(x_rows[:, t, :], src).then_inc(s[f"xin{t}"], 16)
            load_ffn(*FFNS[0], True)
            with sp.Fori(0, KT - 1) as j:
                for k in range(2):
                    load(k, U_LRU, 2, j, cols(W_IN, j * P + k * COL_GATE))
            for k, c in enumerate(((KT - 1) * P, COL_DT, (KT - 1) * P + COL_GATE)):
                load(k, U_LRU, 2, KT - 1, cols(W_IN, c))
            with sp.Fori(0, GROUPS) as g:
                for k in range(PAIRS):
                    load(k, U_GRP, GRP_UNITS, g, cols(W_IN, g * 512 + (COL_XBC + k * P)))
                for k in range(2):
                    load(4 + k, U_GRP, GRP_UNITS, g, cols(W_IN, g * P + (COL_XBC + D_INNER + k * 512)))
                for k in range(PAIRS):
                    load(UG_Z + k, U_GRP, GRP_UNITS, g, cols(W_IN, g * 512 + (COL_Z + k * P)))
                for f in range(4):
                    m, kind = divmod(f, 2)
                    load(UG_MIX + f, U_GRP, GRP_UNITS, g, cols(W_IN, g * 256 + (COL_MIX + kind * D_MODEL + m * P)))
                for r in range(4):
                    src = w_br_ssd[0][bass.ds(g * 512, 512), 256 * r:256 * (r + 1)].rearrange("(k p) c -> p k c", p=P)
                    load(UG_BR + r, U_GRP, GRP_UNITS, g, src, wide=True)
            sp.wait_ge(s["gate_out"], GROUPS * 64)
            with sp.Fori(1, KT // 2 + 1) as i1:
                for m in range(2):
                    load(m, U_MRG - 2, 2, i1, cols(w_br_lru[0], i1 * 256 + (m * P - 256)))
                for m in range(2):
                    sp.wait_ge(s["mg_v"], i1 * 2 + (m - 1))
                    sp.dma_start(gates[:, m, :], gate_spill[bass.ds(i1 * 2 + (m - 2), 1)].rearrange(
                        "o p t -> p (o t)")).then_inc(s[f"gate_in{m}"], 16)
            with sp.Fori(0, KT // 2) as i:
                for k in range(2):
                    load(k, U_OUT, 2, i, cols(w_out[0], i * 256 + k * P))
            load_ffn(*FFNS[1], False)
            for t in range(NT):
                sp.wait_ge(s["out_free"], O_FIN + t + 1)
                dst = y_prompt[0, t * P:(t + 1) * P, :] if t < NT - 1 else y_sample.rearrange("b l d -> (b l) d")
                sp.dma_start(dst, y_out[:, t % 2, :]).then_inc(s["y_dma"], 16)
                if t < NT - 1:
                    sp.wait_ge(s["y_dma"], 16 * (t + 1))
            sp.wait_ge(s["y_dma"], 16 * NT)

        @block.gpsimd
        def _(pool):
            steps = [0]

            def chain(ins):
                steps[0] += 1
                ins.then_inc(s["const"], 1)
                pool.wait_ge(s["const"], steps[0])

            chain(pool.memset(ident[:, :], 0.0))
            chain(pool.affine_select(out=ident[:, :], in_=ident[:, :], compare_op=ALU.not_equal, fill=1.0,
                                     base=0, pattern=[[-1, P]], channel_multiplier=1))
            chain(pool.memset(ones[:, :], 1.0))
            chain(pool.memset(le_mask[:, :, :], 1.0))
            chain(pool.memset(gt_mask[:, :, :], 1.0))
            chain(pool.memset(seq_mask[:, :], 1.0))
            chain(pool.memset(sel[:, :, :], 0.0))
            for m in range(2):
                chain(pool.affine_select(out=le_mask[:, m, :], in_=le_mask[:, m, :], compare_op=ALU.is_ge,
                                         fill=0.0, base=0, pattern=[[1, P]], channel_multiplier=-1))
                chain(pool.affine_select(out=gt_mask[:, m, :], in_=gt_mask[:, m, :], compare_op=ALU.is_ge,
                                         fill=0.0, base=-1, pattern=[[-1, P]], channel_multiplier=1))
            for mask, inner in ((sampled(le_mask[:, 1, :]), [[0, DEC_L]]), (sampled(gt_mask[:, 1, :]), [[0, DEC_L]]),
                                (seq_mask[:, :], [])):
                chain(pool.affine_select(out=mask, in_=mask, compare_op=ALU.is_ge, fill=0.0, base=0,
                                         pattern=[[-DEC_L, DEC_B]] + inner, channel_multiplier=1))
                chain(pool.affine_select(out=mask, in_=mask, compare_op=ALU.is_ge, fill=0.0, base=DEC_L - 1,
                                         pattern=[[DEC_L, DEC_B]] + inner, channel_multiplier=-1))
            v4 = sel[:, :, :].rearrange("h q (two p) -> h q two p", two=2)
            chain(pool.affine_select(out=v4, in_=v4, compare_op=ALU.not_equal, fill=1.0, base=0,
                                     pattern=[[-2, PAIRS], [-1, 2], [0, HD]], channel_multiplier=1))
            assert steps[0] == N_CONST, steps

            pool.wait_ge(s["out_free"], O_LRU)
            pool.dma_start(x_spill, resid[:, :, :].rearrange("p k t -> p (k t)")).then_inc(s["spill"], 16)
            pool.memset(ext[:, 0:HIST], 0.0).then_inc(s["hist_in"], 1)
            pool.memset(acc_ssd[:, 0, :], 0.0).then_inc(s["htail_in"], 1)
            pool.memset(acc_ssd[:, 1:KT, :], 0.0).then_inc(s["acc_zero"], 1)

            def history(n, c):
                pool.wait_ge(s["conv"], n * 7 + 1)
                dst = ext[:, EXT_P:EXT].rearrange("p (b c) -> p b c", b=DEC_B)[:, :, 0:HIST]
                src = tail[:, bass.ds(c, 1), HIST:TAIL].rearrange("p o (b w) -> p (o b) w", b=DEC_B)
                pool.tensor_copy(dst, src).then_inc(s["hist_in"], 1)

            def last_rows(n, c):
                pool.wait_ge(s["ext_in"], n * 3 + 3)
                dst = tail[:, bass.ds(c, 1), :].rearrange("p o w -> p (o w)")
                pool.tensor_copy(dst[:, 0:HIST], ext[:, SEQ:EXT_P]).then_inc(s["tail_in"], 1)
                src = ext[:, EXT_P:EXT].rearrange("p (b c) -> p b c", b=DEC_B)[:, :, DEC_L:DEC_L + HIST]
                pool.tensor_copy(dst[:, HIST:TAIL].rearrange("p (b w) -> p b w", b=DEC_B), src).then_inc(s["tail_in"], 1)
                pool.wait_ge(s["tail_in"], n * 2 + 2)

            def lru_front(j):
                pool.wait_ge(s["gates_mm"], j + 1)
                pool.dma_start(w_gates[:, 0, :], lru_w_rg[0, bass.ds(j, 1)].rearrange("o i j -> i (o j)")).then_inc(s["wg_in"], 16)
                pool.dma_start(w_gates[:, 1, :], lru_w_ig[0, bass.ds(j, 1)].rearrange("o i j -> i (o j)")).then_inc(s["wg_in"], 16)
                history(j, j)
                last_rows(j, j)

            def lru_tails(j):
                pool.wait_ge(s["lru_v"], j * LV + LV_SCAN)
                dst = h_tail[:, bass.ds(j, 1), :].rearrange("p o b -> p (o b)")
                pool.tensor_copy(dst[:, 0:1], h_seq[:, SEQ - 1:SEQ]).then_inc(s["htail_in"], 1)
                pool.tensor_copy(dst[:, 1:1 + DEC_B], h_seq[:, SEQ + DEC_L - 1:TOK:DEC_L]).then_inc(s["htail_in"], 1)

            lru_front(0)
            with pool.Fori(0, KT - 1) as j:
                lru_front(j + 1)
                lru_tails(j)
            lru_tails(KT - 1)

            pool.wait_ge(s["dt_v"], DT_V)
            pool.wait_ge(s["dt_a"], DT_A)
            pool.dma_start(e_spill, e_row[:, :]).then_inc(s["e_out"], 16)
            pool.wait_ge(s["e_out"], 16)
            with pool.Fori(0, GROUPS) as g:
                pool.wait_ge(s["out_free"], g * GRP_OUTS + O_GRP)
                pool.dma_start(e_g[:, :], e_spill[bass.ds(g * HPG, HPG), :]).then_inc(s["eg_in"], 16)
                with nc.allow_non_contiguous_dma(reason="one number per head"):
                    pool.dma_start(d_g[:, :], ssd_D[0, bass.ds(g * HPG, HPG)].rearrange("(h o) -> h o", o=1)).then_inc(s["eg_in"], 16)
                pool.memset(ht[:, :, :], 0.0).then_inc(s["ht_zero"], 1)

                def load_state(qq):
                    for a in range(2):
                        pool.dma_start(h0[qq][:, a, :, :], h_src[bass.ds(g * PAIRS + (2 * qq + a), 1)].rearrange(
                            "o r b n -> r (o b) n")).then_inc(s[f"h0_in{qq}"], 16)

                load_state(0)
                for q in range(PAIRS + 2):
                    n = g * 6 + (KT + q)
                    c = g * PAIRS + (KT + q) if q < PAIRS else g + (KT + 16 + 4 * (q - PAIRS))
                    history(n, c)
                    last_rows(n, c)
                for t in range(NT):
                    if t > 0:
                        pool.wait_ge(s["ssd_p"], g * SP_GRP + (SP * (t - 1) + SP_SEG))
                    le = le_mask[:, t // (NT - 1), :].unsqueeze(1).to_broadcast([P, HPG, P])
                    for part, dst in ((da_hr, m_hi), (da_lo, m_lo)):
                        col = part[:, t, bass.ds(g * HPG, HPG)]
                        if part is da_hr:
                            col = col.bitcast(F32)
                        pool.tensor_tensor(dst[:, :, :], col.unsqueeze(2).to_broadcast([P, HPG, P]), le,
                                           ALU.mult).then_inc(s["m_built"], 1)
                pool.wait_ge(s["ssd_p"], g * SP_GRP + (SP * (NT - 1) + SP_SEG))
                load_state(1)
                pool.wait_ge(s["ssd_a"], g * (SA * NT) + (SA * (NT - 1) + SA_BT))
                pool.tensor_tensor(b_seq[:, :, :], b_tok[:, :].unsqueeze(1).to_broadcast([P, DEC_B, NS]),
                                   seq_mask[:, :].unsqueeze(2).to_broadcast([P, DEC_B, NS]),
                                   ALU.mult).then_inc(s["bseq"], 1)
                pool.wait_ge(s["hs_out"], g * 64 + 64)
                pool.wait_ge(s["hp_out"], g * 16 + 16)
                pool.wait_ge(s["gate_out"], g * 64 + 48)

            pool.wait_ge(s["out_free"], O_TAIL)
            pool.dma_start(x_res[:, :, :].rearrange("p k t -> p (k t)"), x_spill).then_inc(s["reload"], 16)
            pool.wait_ge(s["out_free"], O_TAIL + TAIL_OUTS)
            pool.dma_start(lru_conv_p[0, 0], tail_rows[0:HIST, 0:D_MODEL]).then_inc(s["tails_out"], 16)
            pool.dma_start(ssd_conv_p[0, 0], tail_rows[0:HIST, D_MODEL:]).then_inc(s["tails_out"], 16)
            pool.dma_start(lru_conv_s[0].rearrange("b w c -> (b w) c"), tail_rows[HIST:TAIL, 0:D_MODEL]).then_inc(s["tails_out"], 16)
            pool.dma_start(ssd_conv_s[0].rearrange("b w c -> (b w) c"), tail_rows[HIST:TAIL, D_MODEL:]).then_inc(s["tails_out"], 16)
            pool.dma_start(lru_h_p[0], htail_rows[0:1, :]).then_inc(s["tails_out"], 16)
            pool.dma_start(lru_h_s[0], htail_rows[1:1 + DEC_B, :]).then_inc(s["tails_out"], 16)
            pool.dma_start(g_fin[:, :], norm_final_g.rearrange("(o d) -> o d", o=1).to_broadcast([P, D_MODEL])).then_inc(s["gfin"], 16)
            pool.wait_ge(s["tails_out"], 96)
            pool.wait_ge(s["gfin"], 16)

        @block.tensor
        def _(pe):
            def open_out(o):
                if not (isinstance(o, int) and o < 2):
                    pe.wait_ge(s["out_free"], o - 1)

            def products(dst, side, tiles, hi, lo, ready=None):
                n, at, ins = 3 * len(tiles), 0, None
                for k, c in tiles:
                    for w, a in ((w_hi, hi), (w_lo, hi), (w_hi, lo)):
                        if ready and w is w_hi and k >= ready[3]:
                            pe.wait_ge(s[ready[0 if a is hi else 1]], ready[2] + (k + 1))
                        for h in range(2):
                            ins = pe.matmul(dst[:, h, :], w[:, side, c, :], a[:, k, h * HALF:(h + 1) * HALF],
                                            start=(at == 0), stop=(at == n - 1))
                        at += 1
                ins.then_inc(s["out_ready"], 1)

            def unit(ub, ob, per_u, per_o, i, hi, lo, nk=KT, ready=None):
                pe.wait_ge(s["w_lo_done"], i * per_u + (ub + 1))
                open_out(i * per_o + ob)
                products(out(ob), ub % 2, [(t, t) for t in range(nk)], hi, lo, ready)

            def norm_sum(sq_end):
                pe.wait_ge(s["sq_added"], sq_end)
                for h in range(2):
                    ins = pe.matmul(pn[0][:, h, 0:HALF], ones[:, :], rvar[:, h * HALF:(h + 1) * HALF],
                                    start=True, stop=True)
                ins.then_inc(s["sq_summed"], 1)

            def ffn(u, o, ci, sq0, xn0):
                norm_sum(sq0 + KT)

                cut = ("xh_done", "xl_done", xn0, 0)
                for gi, n, uu, ou, cc, ud, od in ffn_plan(u, o, ci):
                    with pe.Fori(0, n) as i:
                        for k in range(2):
                            unit(uu + k, ou + k, 2, 2, i, act_hi, act_lo,
                                 ready=cut if gi == 0 and k == 0 else None)

                    hidden = ("ff_hi", "ff_lo", cc, n - 2)
                    with pe.Fori(0, KT // 2) as i:
                        for k in range(2):
                            unit(ud + k, od + k, 2, 2, i, h_hi, h_lo, n, ready=hidden if k == 0 else None)

            pe.wait_ge(s["const"], N_CONST)
            for o in range(2 * NT):
                if o % 2 == 0:
                    pe.wait_ge(s[f"xin{o // 2}"], 16)
                open_out(o)
                for k in range(4):
                    ins = pe.transpose(pu[o % 2][:, 0, k * P:(k + 1) * P],
                                       x_rows[:, o // 2, (4 * (o % 2) + k) * P:(4 * (o % 2) + k + 1) * P], ident[:, :])
                ins.then_inc(s["out_ready"], 1)
            pe.wait_ge(s["params"], 16 * N_PARAMS)
            open_out(2 * NT)
            for c in range(CONV_TILES):
                ins = pe.transpose(pu[0][:, c // 16, (c % 16) * 24:(c % 16) * 24 + 24],
                                   hist_rows[:, c * P:(c + 1) * P], ident[0:24, 0:24])
            ins.then_inc(s["out_ready"], 1)
            open_out(2 * NT + 1)
            pe.transpose(pu[1][:, 0, 0:P], vec_rows[:, 0, :], ident[:, :]).then_inc(s["gates_mm"], 1)
            pe.transpose(pu[1][:, 0, P:P + V_SET1], vec_rows[0:V_SET1, 1, :], ident[0:V_SET1, 0:V_SET1])
            for c in range(KT):
                ins = pe.transpose(pu[1][:, 1, c * DEC_B:(c + 1) * DEC_B], h0_rows[:, c * P:(c + 1) * P],
                                   ident[0:DEC_B, 0:DEC_B])
            ins.then_inc(s["out_ready"], 1)

            ffn(U_FFN1, O_FFN1, 0, SQ_FFN1, XN_FFN1)

            norm_sum(SQ_MIX + KT)
            def lru_gates(j):
                pe.wait_ge(s["wg_in"], j * 32 + 32)
                pe.wait_ge(s["conv"], j * 7 + 8)
                for w in range(2):
                    for h in range(2):
                        ins = pe.matmul(pn[w][:, h, 0:HALF], w_gates[:, w, :], xc[:, h * HALF:(h + 1) * HALF],
                                        start=True, stop=True)
                ins.then_inc(s["gates_mm"], 1)

            with pe.Fori(0, KT - 1) as j:
                for k in range(2):
                    unit(U_LRU + k, O_LRU + k, 2, 2, j, act_hi, act_lo,
                         ready=("xh_done", "xl_done", XN_MIX, 0) if k == 0 else None)
                lru_gates(j)

            for k in range(3):
                unit(U_LRU + k, O_LRU + k, 2, 2, KT - 1, act_hi, act_lo)
            pe.wait_ge(s["conv"], 7 * KT + 1)
            pe.wait_ge(s["dt_v"], 12)
            for kind, row in enumerate((dt_row, da_row)):
                for t in range(NT):
                    c = (kind * NT + t) * HEADS
                    ins = pe.transpose(pn[0][:, 0, c:c + HEADS], row[:, t * P:(t + 1) * P], ident[0:HEADS, 0:HEADS])
            ins.then_inc(s["dt_p"], 1)
            pe.wait_ge(s["dt_v"], 14)
            for t in range(NT):
                pe.matmul(pn[1][:, 0, t * HEADS:(t + 1) * HEADS], gt_mask[:, t // (NT - 1), :], da_col[:, t, :],
                          start=True, stop=True)
            pe.matmul(pn[1][:, 1, 0:(NT - 1) * HEADS], ones[:, :],
                      da_col[:, 0:NT - 1, :].rearrange("p t h -> p (t h)"),
                      start=True, stop=True).then_inc(s["dt_p"], 1)
            pe.wait_ge(s["dt_a"], DT_A)
            lru_gates(KT - 1)
            pe.wait_ge(s["gtr"], 1)

            with pe.Fori(0, GROUPS) as g:
                def grp_unit(k, nk=KT):
                    unit(U_GRP + k, O_GRP + k, GRP_UNITS, GRP_OUTS, g, act_hi, act_lo)

                def sv(t, step):
                    pe.wait_ge(s["ssd_v"], g * SV_GRP + (SV * t + step))

                def scores(t):
                    tile = slice(t * P, (t + 1) * P)
                    if t == 0:
                        pe.wait_ge(s["xb_out"], g * 6 + 6)
                    else:
                        sv(t - 1, SV_T2)
                    for q in range(PAIRS):
                        ins = pe.transpose(pn[0][:, 0, q * P:(q + 1) * P], xf[:, q, tile], ident[:, :])
                    ins.then_inc(s["ssd_p"], 1)
                    pe.transpose(pn[0][:, 1, 0:P], xf[:, PAIRS, tile], ident[:, :])
                    pe.matmul(pn[0][:, 1, P:2 * P], xf[:, PAIRS, tile], xf[:, PAIRS + 1, tile],
                              start=True, stop=True).then_inc(s["ssd_p"], 1)
                    pe.wait_ge(s["m_built"], g * (2 * NT) + (2 * t + 2))
                    if t == 0:
                        pe.wait_ge(s["eq_cp"], g + 1)
                    elif t < NT - 1:
                        sv(t - 1, SV_H1)
                    else:
                        pe.wait_ge(s["hp_cp"], g + 1)
                    for b in range(2):
                        for part, m in enumerate((m_hi, m_lo)):
                            ins = pe.matmul(pn[1][:, b, :], gt_r[:, t // (NT - 1), :],
                                            m[:, 4 * b:4 * b + 4, :].rearrange("p h l -> p (h l)"),
                                            start=(part == 0), stop=(part == 1))
                    ins.then_inc(s["ssd_p"], 1)

                def inner(t):
                    sv(t, SV_G)
                    for h in range(HPG):
                        r = HD * (h % 2)
                        ins = pe.matmul(pn[0][r:r + HD, 0, (h // 2) * P:(h // 2 + 1) * P], xd[:, h, :], lmat[:, h, :],
                                        start=True, stop=True)
                    ins.then_inc(s["ssd_p"], 1)
                    for q in range(PAIRS):
                        ins = pe.matmul(pn[1][:, 0, q * P:(q + 1) * P], sel[:, q, :], e_g[:, t * P:(t + 1) * P],
                                        start=True, stop=True)
                    ins.then_inc(s["ssd_p"], 1)

                def gate_unit(f):
                    unit(U_GRP + UG_MIX + f, O_GRP + OG_MIX[f], GRP_UNITS, GRP_OUTS, g, act_hi, act_lo)

                for k in range(PAIRS + 2):
                    grp_unit(k)
                pe.wait_ge(s["eg_in"], g * 32 + 32)
                for q in range(PAIRS):
                    c = q * (DEC_B + 1)
                    pe.matmul(pn[1][:, 0, c:c + DEC_B], sel[:, q, :], e_g[:, SEQ + DEC_L - 1:TOK:DEC_L],
                              start=True, stop=True)
                    ins = pe.matmul(pn[1][:, 0, c + DEC_B:c + DEC_B + 1], sel[:, q, :], d_g[:, :],
                                    start=True, stop=True)
                ins.then_inc(s["eq_mm"], 1)
                grp_unit(UG_Z)
                for t in range(NT - 1):
                    scores(t)
                    if t < NT - 2:
                        grp_unit(UG_Z + t + 1)
                    else:
                        gate_unit(0)
                    inner(t)
                    if t == 0:
                        pe.wait_ge(s["ht_zero"], g + 1)
                    for q in range(PAIRS):
                        ins = pe.matmul(pn[0][:, 1, q * P:(q + 1) * P],
                                        ht[:, 2 * q:2 * q + 2, :].rearrange("n a b -> n (a b)"),
                                        xf[:, PAIRS + 1, t * P:(t + 1) * P], start=True, stop=True)
                    ins.then_inc(s["ssd_p"], 1)
                    pe.matmul(pn[1][:, 1, :], b_tok[:, :], xdd[:, :, :].rearrange("p h d -> p (h d)"),
                              start=True, stop=True).then_inc(s["ssd_p"], 1)
                sv(NT - 2, SV_H1)
                for q in range(PAIRS):
                    ins = pe.transpose(pn[1][:, 1, q * P:(q + 1) * P],
                                       ht[:, 2 * q:2 * q + 2, :].rearrange("n a b -> n (a b)"), ident[:, :])
                ins.then_inc(s["hp_mm"], 1)

                def old_states(qq):
                    pe.wait_ge(s[f"h0_in{qq}"], g * 32 + 32)
                    for a in range(2):
                        o = O_GRP + OG_OLD[qq] + a
                        open_out(g * GRP_OUTS + o)
                        for b in range(DEC_B):
                            ins = pe.transpose(pu[o % 2][:, b // 4, (b % 4) * P:(b % 4 + 1) * P], h0[qq][:, a, b, :], ident[:, :])
                        ins.then_inc(s["out_ready"], 1)

                def from_states(qq):
                    for a in range(2):
                        q = 2 * qq + a
                        pe.wait_ge(s["out_free"], g * GRP_OUTS + (O_GRP + OG_OLD[qq] + a + 1))
                        for b in range(DEC_B):
                            c = SEQ + b * DEC_L
                            ins = pe.matmul(pn[0][:, 1, q * P + b * DEC_L:q * P + (b + 1) * DEC_L], h0_t[:, a, b, :],
                                            xf[:, PAIRS + 1, c:c + DEC_L], start=True, stop=True)
                    return ins

                def new_states(qq):
                    for a in range(2):
                        o = O_GRP + OG_NEW[qq] + a
                        open_out(g * GRP_OUTS + o)
                        q = 2 * qq + a
                        for b in range(2):
                            ins = pe.matmul(pu[o % 2][:, b, :], xdd[:, 2 * q:2 * q + 2, :].rearrange("p h d -> p (h d)"),
                                            b_seq[:, 4 * b:4 * b + 4, :].rearrange("p b n -> p (b n)"),
                                            start=True, stop=True)
                        ins.then_inc(s["out_ready"], 1)

                scores(NT - 1)
                old_states(0)
                gate_unit(1)
                inner(NT - 1)
                from_states(0)
                old_states(1)
                pe.wait_ge(s["bseq"], g + 1)
                new_states(0)
                from_states(1).then_inc(s["ssd_p"], 1)
                new_states(1)
                gate_unit(2)
                norm_sum(g * SQG + (SQ_GRP + SQG))
                gate_unit(3)
                for r in range(4):
                    pe.wait_ge(s["w_lo_done"], g * GRP_UNITS + (U_GRP + UG_BR + r + 1))
                    for m in range(2):
                        o = O_GRP + OG_BR + 2 * r + m
                        open_out(g * GRP_OUTS + o)
                        products(out(o), (U_GRP + UG_BR + r) % 2, [(k, 2 * k + m) for k in range(PAIRS)], yn_hi, yn_lo,
                                 ready=("xh_done", "xl_done", g * PAIRS + XN_GRP, 0)
                                 if r == 0 and m == 0 else None)

            with pe.Fori(0, KT // 2) as i:
                for m in range(2):
                    unit(U_MRG + m, O_MRG + m, 2, 2, i, yl_hi, yl_lo,
                         ready=("yl_hi_done", "yl_lo_done", 0, 0) if m == 0 else None)
            for a in range(4):
                o = O_TAIL + a
                open_out(o)
                for b in range(8):
                    ins = pe.transpose(pu[o % 2][0:TAIL, b // 4, (b % 4) * P:(b % 4 + 1) * P], tail[:, 8 * a + b, :], ident[:, :])
                ins.then_inc(s["out_ready"], 1)
            o = O_TAIL + 4
            open_out(o)
            for b in range(KT):
                ins = pe.transpose(pu[o % 2][0:1 + DEC_B, b // 4, (b % 4) * P:(b % 4 + 1) * P], h_tail[:, b, :], ident[:, :])
            ins.then_inc(s["out_ready"], 1)
            with pe.Fori(0, KT // 2) as i:
                for k in range(2):
                    unit(U_OUT + k, O_OUT + k, 2, 2, i, act_hi, act_lo,
                         ready=("mh_done", "ml_done", 0, 0) if k == 0 else None)
            ffn(U_FFN2, O_FFN2, 22, SQ_FFN2, XN_FFN2)

            pe.wait_ge(s["out_free"], O_FIN)
            for t in range(NT):
                o = O_FIN + t
                open_out(o)
                for k in range(KT):
                    ins = pe.transpose(pu[o % 2][:, k // 4, (k % 4) * P:(k % 4 + 1) * P], resid[:, k, t * P:(t + 1) * P], ident[:, :])
                ins.then_inc(s["out_ready"], 1)

        @block.scalar
        def _(act):
            def cut_weights(u, per, i):
                side = u % 2
                act.wait_ge(s[f"w_in{side}"], i * (8 * per) + 16 * (u // 2 + 1))
                act.activation(w_hi[:, side, :, :], w_raw[:, side, :, :], ACT.Copy).then_inc(s["w_hi_done"], 1)

            def take(u, o, per_u, per_o, i):
                act.wait_ge(s["out_ready"], i * per_o + (o + 1))
                cut_weights(u + 2, per_u, i)

            def square_tile(sq, side, src, dst=None):
                if not (isinstance(sq, int) and sq < 2):
                    act.wait_ge(s["sq_added"], sq - 1)
                act.activation(dst or squares[:, side, 0:src.shape[1]], src, ACT.Square).then_inc(s["sq_done"], 1)

            def norm_rstd(n, scale):
                act.activation(ln_col[:, :], eps_col[:, :], ACT.Ln).then_inc(s["ln_ready"], 1)
                act.wait_ge(s["ln_ready"], n + 1)
                act.wait_ge(s["sq_summed"], n + 1)
                act.activation(halves(rtmp[:, :]), pn[0][:, :, 0:HALF], ACT.Ln, scale=scale,
                               bias=eps_col[:, 0:1]).then_inc(s["rs_act"], 1)
                act.wait_ge(s["rs_act"], n * 2 + 1)
                act.activation(rstd[:, :], rtmp[:, :], ACT.Exp, scale=-0.5).then_inc(s["rs_act"], 1)

            def norm_cut(xn0, count, hi):
                for k in range(count):
                    act.wait_ge(s["xn_done"], xn0 + (k + 1))
                    act.activation(hi[:, k, :], squares[:, k % 2, :], ACT.Copy).then_inc(s["xh_done"], 1)

            def ffn(u, o, ci, n_norm, xn0, final):
                norm_rstd(n_norm, 1.0 / D_MODEL)
                norm_cut(xn0, KT, act_hi)
                if not final:
                    lru_decay()
                for gi, n, uu, ou, cc, ud, od in ffn_plan(u, o, ci):
                    with act.Fori(0, n) as i:
                        take(uu, ou, 2, 2, i)
                        act.activation(halves(ff_t[:, :]), out(ou), ACT.Tanh, scale=0.5).then_inc(s["ff_th"], 1)
                        take(uu + 1, ou + 1, 2, 2, i)
                        act.wait_ge(s["out_free"], i * 2 + (ou + 2))
                        act.activation(feature_tile(h_hi, i), ff_h[:, :], ACT.Copy).then_inc(s["ff_hi"], 1)
                    last = final and gi == len(FFN_GROUPS) - 1
                    with act.Fori(0, KT // 2 - (1 if last else 0)) as i:
                        for k in range(2):
                            take(ud + k, od + k, 2, 2, i)
                            if gi == len(FFN_GROUPS) - 1 and not final:
                                act.wait_ge(s["out_free"], i * 2 + (od + k + 1))
                                square_tile(i * 2 + (SQ_MIX + k), k, feature_tile(resid, i * 2 + k))

            rows = [(ssd_conv_w[0].rearrange("w (k p) -> (w k) p", p=P), 0, 0),
                    (ssd_conv_b[0].rearrange("(k p) -> k p", p=P), 0, V_SCB),
                    (lru_conv_b[0].rearrange("(k p) -> k p", p=P), 0, V_LCB),
                    (lru_conv_w[0].rearrange("w (k p) -> (w k) p", p=P), 1, V_LCW - 128)]
            for w, c in ((lru_b_rg, V_BR), (lru_b_ig, V_BI), (lru_lambda, V_LAM), (norm_ffn1_g, V_NF1),
                         (norm_mix_g, V_NMIX), (norm_ffn2_g, V_NF2), (ssd_norm_g, V_SNG), (b_gate, V_BG)):
                rows.append((w[0].rearrange("(k p) -> k p", p=P), 1, c - 128))
            for src, t, r in rows:
                act.dma_start(vec_rows[r:r + src.shape[0], t, :], src).then_inc(s["params"], 16)
            act.dma_start(hist_rows[:, 0:D_MODEL], state_lru_conv[0].rearrange("b w c -> (b w) c")).then_inc(s["params"], 16)
            act.dma_start(hist_rows[:, D_MODEL:], state_ssd_conv[0].rearrange("b w c -> (b w) c")).then_inc(s["params"], 16)
            act.dma_start(h0_rows[:, :], state_lru_h[0]).then_inc(s["params"], 16)
            with nc.allow_non_contiguous_dma(reason="one number per head"):
                act.dma_start(head_vec[:, 0:1], ssd_dt_bias[0].rearrange("(h o) -> h o", o=1)).then_inc(s["params"], 16)
                act.dma_start(head_vec[:, 1:2], ssd_A_log[0].rearrange("(h o) -> h o", o=1)).then_inc(s["params"], 16)
            assert len(rows) + 5 == N_PARAMS

            act.wait_ge(s["const"], N_CONST)
            cut_weights(0, 2, 0)
            cut_weights(1, 2, 0)
            def lru_decay():
                lam = vec[:, V_LAM:V_LAM + KT]
                act.wait_ge(s["start_v"], 1)
                act.activation(lam_t[:, 0, :], lam, ACT.Abs).then_inc(s["start_a"], 1)
                act.wait_ge(s["start_a"], 1)
                act.activation(lam_t[:, 1, :], lam_t[:, 0, :], ACT.Exp, scale=-1.0).then_inc(s["start_a"], 1)
                act.wait_ge(s["start_v"], 2)
                act.activation(lam_t[:, 3, :], lam_t[:, 2, :], ACT.Ln).then_inc(s["start_a"], 1)

            act.wait_ge(s["out_free"], 2 * NT)
            for k in range(KT):
                square_tile(SQ_FFN1 + k, k % 2, resid[:, k, :])
            ffn(U_FFN1, O_FFN1, 0, 0, XN_FFN1, False)

            norm_rstd(1, 1.0 / D_MODEL)
            norm_cut(XN_MIX, KT, act_hi)

            def to_ext(o, per_o, i, n):
                act.wait_ge(s["hist_in"], n + 2)
                act.activation(ext[:, HIST:HIST + HALF], pu[o % 2][:, 0, 0:HALF], ACT.Copy).then_inc(s["ext_in"], 1)
                act.activation(ext[:, HIST + HALF:EXT_P], pu[o % 2][:, 1, 0:SEQ - HALF], ACT.Copy).then_inc(s["ext_in"], 1)
                act.activation(ext[:, EXT_P:EXT].rearrange("p (b c) -> p b c", b=DEC_B)[:, :, HIST:],
                               sampled(pu[o % 2][:, 1, SEQ - HALF:HALF]), ACT.Copy).then_inc(s["ext_in"], 1)

            def lru_front(j):
                take(U_LRU, O_LRU, 2, 2, j)
                to_ext(O_LRU, 2, j, j)

            def lru_head(j, last=False):
                def lv(step):
                    act.wait_ge(s["lru_v"], j * LV + step)

                def la(step):
                    act.wait_ge(s["lru_a"], j * LA + step)

                r = 2 if last else 1
                take(U_LRU + r, O_LRU + r, 2, 2, j)
                act.activation(halves(g_2[:, :]), out(O_LRU + r), ACT.Square).then_inc(s["lru_a"], 1)
                act.wait_ge(s["gates_mm"], j + 2)
                act.activation(halves(t_r[:, :]), pn[0][:, :, 0:HALF], ACT.Tanh, scale=0.5,
                               bias=v(j + V_BR)).then_inc(s["lru_a"], 1)
                lv(LV_P)
                act.activation(halves(t_i[:, :]), pn[1][:, :, 0:HALF], ACT.Tanh, scale=0.5,
                               bias=v(j + V_BI)).then_inc(s["lru_a"], 1)
                lv(LV_Q)
                act.activation(g_t[:, :], g_q[:, :], ACT.Tanh, scale=GELU_C).then_inc(s["lru_a"], 1)
                lv(LV_LA)
                act.activation(l_a[:, :], t_r[:, :], ACT.Exp).then_inc(s["lru_a"], 1)
                act.activation(l_t2[:, :], t_r[:, :], ACT.Tanh).then_inc(s["lru_a"], 1)
                la(LA_A)
                act.activation(l_a2[:, :], l_a[:, :], ACT.Square).then_inc(s["lru_a"], 1)
                if not last:
                    lru_front(j + 1)
                lv(LV_V)
                act.activation(l_u[:, :], l_t2[:, :], ACT.Sqrt, scale=-1.0).then_inc(s["lru_a"], 1)

            lru_front(0)
            with act.Fori(0, KT - 1) as j:
                lru_head(j)
            take(U_DT, O_DT, 1, 1, 0)
            act.wait_ge(s["out_free"], O_DT + 1)
            act.activation(dt_e[:, :], dt_x[:, :], ACT.Abs).then_inc(s["dt_a"], 1)
            act.wait_ge(s["dt_a"], 1)
            act.activation(dt_e[:, :], dt_e[:, :], ACT.Exp, scale=-1.0).then_inc(s["dt_a"], 1)
            act.activation(head_vec[:, 2:3], head_vec[:, 1:2], ACT.Exp).then_inc(s["dt_a"], 1)
            act.wait_ge(s["dt_v"], 4)
            act.activation(dt_l[:, :], dt_w[:, :], ACT.Ln).then_inc(s["dt_a"], 1)
            act.wait_ge(s["dt_v"], 12)
            act.activation(e_row[:, :], e_row[:, :], ACT.Exp).then_inc(s["dt_a"], 1)
            act.wait_ge(s["dt_v"], 14)
            act.activation(da_hr[:, :, :], da_col[:, :, :], ACT.Copy).then_inc(s["dt_a"], 1)
            act.wait_ge(s["dt_p"], 2)
            act.activation(dd_col[:, :, :].rearrange("p t h -> p (t h)"), pn[1][:, 0, 0:NT * HEADS], ACT.Exp).then_inc(s["dt_a"], 1)
            act.activation(e_tot[:, :, :].rearrange("p t h -> p (t h)"), pn[1][:, 1, 0:(NT - 1) * HEADS], ACT.Exp).then_inc(s["dt_a"], 1)

            lru_head(KT - 1, True)

            with act.Fori(0, GROUPS) as g:
                def silu_z(q):
                    k = UG_Z + q
                    take(U_GRP + k, O_GRP + k, GRP_UNITS, GRP_OUTS, g)
                    act.wait_ge(s["out_free"], g * GRP_OUTS + (O_GRP + k))
                    act.activation(halves(rtmp[:, :]), out(O_GRP + k), ACT.Tanh, scale=0.5).then_inc(s["z_th"], 1)

                def gate(f):
                    m, kind = divmod(f, 2)
                    o = O_GRP + OG_MIX[f]
                    take(U_GRP + UG_MIX + f, o, GRP_UNITS, GRP_OUTS, g)
                    act.wait_ge(s["out_free"], g * GRP_OUTS + o)
                    if f > 0:
                        act.wait_ge(s["gate_out"], g * 64 + 16 * f)
                    act.activation(halves(gate_buf[f]), out(o), ACT.Tanh, scale=0.5,
                                   bias=v(g * 2 + (V_BG + kind * KT + m))).then_inc(s["gate_th"], 1)

                def gate_store(f):
                    m, kind = divmod(f, 2)
                    act.wait_ge(s["out_free"], g * GRP_OUTS + (O_GRP + OG_MIX[f] + 1))
                    act.dma_start(gate_spill[bass.ds(g * 2 + m, 1), :, kind * TOK:(kind + 1) * TOK].rearrange(
                        "o p t -> p (o t)"), gate_buf[f]).then_inc(s["gate_out"], 16)

                for k in range(PAIRS + 2):
                    take(U_GRP + k, O_GRP + k, GRP_UNITS, GRP_OUTS, g)
                    to_ext(O_GRP + k, GRP_OUTS, g, g * 6 + (KT + k))
                    act.wait_ge(s["conv"], g * 42 + (7 * (KT + k + 1) + 1))
                    act.activation(rtmp[:, :], xf[:, k, :], ACT.Tanh).then_inc(s["xb_th"], 1)
                act.wait_ge(s["xb_out"], g * 6 + 6)
                silu_z(0)
                for t in range(NT):
                    act.wait_ge(s["ssd_p"], g * SP_GRP + (SP * t + SP_CB))
                    act.activation(b_tok[:, :], pn[0][:, 1, 0:P], ACT.Copy).then_inc(s["ssd_a"], 1)
                    act.wait_ge(s["ssd_p"], g * SP_GRP + (SP * t + SP_SEG))
                    act.activation(lmat[:, :, :].rearrange("p (b h) l -> p b (h l)", b=2), pn[1][:, :, :],
                                   ACT.Exp).then_inc(s["ssd_a"], 1)
                    if t < NT - 2:
                        silu_z(t + 1)
                    elif t == NT - 2:
                        gate(0)
                    else:
                        for k in range(PAIRS):
                            act.wait_ge(s["yz"], g * SQG + (k + 1))
                            square_tile(g * SQG + (SQ_GRP + k), k % 2, xf[:, k, 0:SEQ])
                        gate(1)
                        gate_store(1)
                    act.wait_ge(s["ssd_p"], g * SP_GRP + (SP * t + SP_E))
                    act.activation(es[:, :], pn[1][:, 0, :], ACT.Copy).then_inc(s["ssd_a"], 1)
                    if t == NT - 2:
                        gate_store(0)
                        act.wait_ge(s["hp_cp"], g + 1)
                        act.dma_start(hp_dst[:, bass.ds(g * PAIRS, PAIRS), :], hp_rows[:, :, :]).then_inc(s["hp_out"], 16)
                for qq in range(2):
                    for a in range(2):
                        act.wait_ge(s["out_free"], g * GRP_OUTS + (O_GRP + OG_NEW[qq] + a + 1))
                        act.dma_start(h_dst[bass.ds(g * PAIRS + (2 * qq + a), 1)].rearrange("o r b n -> r (o b) n"),
                                      h0[qq][:, a, :, :]).then_inc(s["hs_out"], 16)
                act.wait_ge(s["yz"], g * SQG + SQG)
                square_tile(g * SQG + (SQ_GRP + PAIRS), 0, xf[:, 0:PAIRS, SEQ:TOK],
                            squares[:, 0, 0:PAIRS * P].rearrange("p (q c) -> p q c", q=PAIRS))
                gate(2)
                gate_store(2)
                norm_rstd(g + 2, 0.25 / 512)
                norm_cut(g * PAIRS + XN_GRP, PAIRS, yn_hi)
                gate(3)
                gate_store(3)
                for r in range(4):
                    take(U_GRP + UG_BR + r, O_GRP + OG_BR + 2 * r + 1, GRP_UNITS, GRP_OUTS, g)
                act.wait_ge(s["gate_out"], g * 64 + 64)

            act.wait_ge(s["out_free"], O_MRG)
            for k in range(KT):
                act.activation(yl_hi[:, k, :], resid[:, k, :], ACT.Copy).then_inc(s["yl_hi_done"], 1)
            with act.Fori(0, KT // 2) as i:
                for m in range(2):
                    take(U_MRG + m, O_MRG + m, 2, 2, i)
                    act.wait_ge(s["mg_v"], i * 2 + (m + 3))
                    act.activation(feature_tile(act_hi, i * 2 + m), feature_tile(resid, i * 2 + m),
                                   ACT.Copy).then_inc(s["mh_done"], 1)
            with act.Fori(0, KT // 2) as i:
                for k in range(2):
                    take(U_OUT + k, O_OUT + k, 2, 2, i)
                    act.wait_ge(s["out_free"], i * 2 + (O_OUT + k + 1))
                    square_tile(i * 2 + (SQ_FFN2 + k), k, feature_tile(resid, i * 2 + k))

            ffn(U_FFN2, O_FFN2, 22, 2 + GROUPS, XN_FFN2, True)

            for t in range(NT):
                act.wait_ge(s["out_ready"], O_FIN + t + 1)
                if t:
                    act.wait_ge(s["fin_a"], 2 * t - 1)
                act.activation(y_sq, pu[(O_FIN + t) % 2][:, :, :], ACT.Square,
                               accum_out=fin[:, 0, t:t + 1]).then_inc(s["fin_a"], 1)
                act.wait_ge(s["fin_v"], 6 * t + 1)
                act.activation(fin[:, 2, t:t + 1], fin[:, 1, t:t + 1], ACT.Sqrt).then_inc(s["fin_a"], 1)

        @block.vector
        def _(dve):
            def stt(dst, a, scalar, b, op0, op1):
                return dve.scalar_tensor_tensor(out=dst, in0=a, scalar=scalar, in1=b, op0=op0, op1=op1)

            def cut_weights(u, per, i):
                side = u % 2
                dve.wait_ge(s["w_hi_done"], i * per + (u + 1))
                dve.tensor_tensor(w_lo[:, side, :, :], w_raw[:, side, :, :], w_hi[:, side, :, :].bitcast(F32),
                                  ALU.subtract).then_inc(s["w_lo_done"], 1)

            def take(u, o, per_u, per_o, i, ahead=True):
                if ahead:
                    cut_weights(u + 2, per_u, i)
                dve.wait_ge(s["out_ready"], i * per_o + (o + 1))

            def clear_sum(n):
                dve.memset(rvar[:, :], 0.0).then_inc(s["sq_clear"], 1)
                dve.wait_ge(s["sq_clear"], n + 1)

            def add_square(sq, side, n=TOK):
                dve.wait_ge(s["sq_done"], sq + 1)
                dve.tensor_tensor(rvar[:, 0:n], rvar[:, 0:n], squares[:, side, 0:n], ALU.add).then_inc(s["sq_added"], 1)
                dve.wait_ge(s["sq_added"], sq + 1)

            def norm(n, xn0, src, count, scale, gain, hi, lo):
                var, r, t = rvar[:, :], rstd[:, :], rtmp[:, :]

                def step(j, ins):
                    ins.then_inc(s["rs_step"], 1)
                    dve.wait_ge(s["rs_step"], n * 4 + j)

                dve.wait_ge(s["rs_act"], n * 2 + 1)
                step(1, dve.tensor_scalar(halves(var), pn[0][:, :, 0:HALF], -0.5 * scale, -0.5 * EPS, ALU.mult, ALU.add))
                dve.wait_ge(s["rs_act"], n * 2 + 2)
                step(2, dve.tensor_tensor(t, var, r, ALU.mult))
                step(3, dve.tensor_tensor(t, t, r, ALU.mult))
                step(4, stt(r, t, 1.5, r, ALU.add, ALU.mult))

                def rest(k):
                    dve.wait_ge(s["xh_done"], xn0 + (k + 1))
                    dve.tensor_tensor(lo[:, k, :], squares[:, k % 2, :], hi[:, k, :].bitcast(F32),
                                      ALU.subtract).then_inc(s["xl_done"], 1)

                for k in range(count):
                    if k >= 2:
                        rest(k - 2)
                        dve.wait_ge(s["xl_done"], xn0 + (k - 1))
                    stt(squares[:, k % 2, :], src[:, k, :], v(gain(k)), r, ALU.mult, ALU.mult).then_inc(s["xn_done"], 1)
                for k in range(count - 2, count):
                    rest(k)

            def ffn(u, o, ci, n_norm, xn0, gain, final):
                norm(n_norm, xn0, resid, KT, 1.0 / D_MODEL, lambda k: gain + k, act_hi, act_lo)
                if not final:
                    lru_decay()
                for gi, n, uu, ou, cc, ud, od in ffn_plan(u, o, ci):
                    with dve.Fori(0, n) as i:
                        take(uu, ou, 2, 2, i)
                        dve.wait_ge(s["ff_th"], i + (cc + 1))
                        stt(halves(ff_a[:, :]), halves(ff_t[:, :]), 1.0, out(ou), ALU.add, ALU.mult).then_inc(s["out_free"], 1)
                        take(uu + 1, ou + 1, 2, 2, i)
                        dve.wait_ge(s["out_free"], i * 2 + (ou + 1))
                        dve.tensor_tensor(halves(ff_h[:, :]), halves(ff_a[:, :]), out(ou + 1), ALU.mult).then_inc(s["out_free"], 1)
                        dve.wait_ge(s["ff_hi"], i + (cc + 1))
                        dve.tensor_tensor(feature_tile(h_lo, i), ff_h[:, :], feature_tile(h_hi, i).bitcast(F32),
                                          ALU.subtract).then_inc(s["ff_lo"], 1)
                    last = final and gi == len(FFN_GROUPS) - 1

                    def down(i, k, ahead=True):
                        take(ud + k, od + k, 2, 2, i, ahead)
                        r = halves(feature_tile(resid, i * 2 + k))
                        stt(r, out(od + k), 0.25, r, ALU.mult, ALU.add).then_inc(s["out_free"], 1)
                        if gi == len(FFN_GROUPS) - 1 and not final:
                            add_square(i * 2 + (SQ_MIX + k), k)

                    if gi == len(FFN_GROUPS) - 1 and not final:
                        clear_sum(1)

                    with dve.Fori(0, KT // 2 - (1 if last else 0)) as i:
                        for k in range(2):
                            down(i, k)
                    if last:
                        for k in range(2):
                            down(KT // 2 - 1, k, False)

            def chained(name, base, ins, j):
                ins.then_inc(s[name], 1)
                dve.wait_ge(s[name], base + j)

            def lru_decay():
                lt = [lam_t[:, k, :] for k in range(8)]
                lam = vec[:, V_LAM:V_LAM + KT]
                dve.wait_ge(s["start_a"], 2)
                chained("start_v", 0, dve.tensor_scalar(lt[2], lt[1], 1.0, None, ALU.add), 2)
                dve.wait_ge(s["start_a"], 3)
                chained("start_v", 0, dve.tensor_scalar(lt[4], lt[2], -1.0, TINY, ALU.add, ALU.add), 3)
                chained("start_v", 0, dve.reciprocal(lt[5], lt[4]), 4)
                chained("start_v", 0, stt(lt[6], lt[3], TINY, lt[1], ALU.add, ALU.mult), 5)
                chained("start_v", 0, dve.tensor_tensor(lt[6], lt[6], lt[5], ALU.mult), 6)
                chained("start_v", 0, dve.tensor_scalar(lt[7], lam, -1.0, 0.0, ALU.mult, ALU.max), 7)
                chained("start_v", 0, dve.tensor_tensor(lt[7], lt[7], lt[6], ALU.add), 8)
                chained("start_v", 0, dve.tensor_scalar(lru_c[:, :], lt[7], -4.0, None, ALU.mult), 9)
                for n, (a, b) in enumerate(((V_SCW, V_SCB + 24), (V_BR, V_BI + KT), (V_SNG, V_BG + 2 * KT))):
                    chained("start_v", 0, dve.tensor_scalar(vec[:, a:b], vec[:, a:b], 0.5, None, ALU.mult), 10 + n)

            dve.memset(eps_col[:, :], EPS).then_inc(s["conv"], 1)
            for k in range(2):
                cut_weights(k, 2, 0)
            dve.wait_ge(s["const"], N_CONST)
            dve.tensor_copy(gt_r[:, :, :], gt_mask[:, :, :]).then_inc(s["gtr"], 1)
            for o in range(2 * NT):
                dve.wait_ge(s["out_ready"], o + 1)
                dve.tensor_copy(resid[:, 4 * (o % 2):4 * (o % 2) + 4, (o // 2) * P:(o // 2 + 1) * P],
                                pu[o % 2][:, 0, :].rearrange("p (k t) -> p k t", k=4)).then_inc(s["out_free"], 1)
            clear_sum(0)
            for k in range(KT):
                add_square(SQ_FFN1 + k, k % 2)
            dve.wait_ge(s["out_ready"], 2 * NT + 1)
            dve.tensor_copy(tail[:, :, HIST:TAIL].rearrange("p (b c) w -> p b c w", b=2),
                            pu[0][:, :, 0:384].rearrange("p b (c w) -> p b c w", c=16)).then_inc(s["out_free"], 1)
            dve.wait_ge(s["out_ready"], 2 * NT + 2)
            chained("start_v", 0, dve.tensor_copy(vec[:, :], pu[1][:, 0, 0:240]), 1)
            dve.tensor_copy(h0_lru[:, :, :].rearrange("p k b -> p (k b)"), pu[1][:, 1, 0:KT * DEC_B]).then_inc(s["out_free"], 1)
            ffn(U_FFN1, O_FFN1, 0, 0, XN_FFN1, V_NF1, False)

            norm(1, XN_MIX, resid, KT, 1.0 / D_MODEL, lambda k: V_NMIX + k, act_hi, act_lo)
            dve.wait_ge(s["spill"], 16)

            def convolve(dst, n, per_o, i, o, w, step, bias):
                dve.wait_ge(s["ext_in"], n * 3 + 3)
                es_ = ext[:, EXT_P:EXT].rearrange("p (b c) -> p b c", b=DEC_B)
                dp, ds = dst[:, 0:SEQ], sampled(dst[:, SEQ:TOK])
                dve.tensor_scalar(dp, ext[:, 0:SEQ], v(w), v(bias), ALU.mult, ALU.add).then_inc(s["out_free"], 1)
                dve.tensor_scalar(ds, es_[:, :, 0:DEC_L], v(w), v(bias), ALU.mult, ALU.add).then_inc(s["conv"], 1)
                for k in range(1, 4):
                    if k == 1:
                        dve.wait_ge(s["out_free"], i * per_o + (o + 1))
                    else:
                        dve.wait_ge(s["conv"], n * 7 + (2 * k - 1))
                    stt(dp, ext[:, k:k + SEQ], v(w + step * k), dp, ALU.mult, ALU.add).then_inc(s["conv"], 1)
                    dve.wait_ge(s["conv"], n * 7 + 2 * k)
                    stt(ds, es_[:, :, k:k + DEC_L], v(w + step * k), ds, ALU.mult, ALU.add).then_inc(s["conv"], 1)

            def lru_front(j):
                take(U_LRU, O_LRU, 2, 2, j)
                convolve(xc, j, 2, j, O_LRU, j + V_LCW, KT, j + V_LCB)

            def lru_head(j, last=False):
                def lv(step):
                    dve.wait_ge(s["lru_v"], j * LV + step)

                def la(step):
                    dve.wait_ge(s["lru_a"], j * LA + step)

                def done(ins):
                    ins.then_inc(s["lru_v"], 1)

                r = 2 if last else 1
                take(U_LRU + r, O_LRU + r, 2, 2, j)
                la(LA_G2)
                done(dve.tensor_scalar(g_q[:, :], g_2[:, :], GELU_A, 1.0, ALU.mult, ALU.add))
                lv(LV_P)
                done(dve.tensor_tensor(halves(g_q[:, :]), halves(g_q[:, :]), out(O_LRU + r), ALU.mult))
                la(LA_TI)
                done(dve.tensor_scalar(t_r[:, :], t_r[:, :], 1.0, lru_c[:, bass.ds(j, 1)], ALU.add, ALU.mult))
                done(stt(t_i[:, :], t_i[:, :], 1.0, xc[:, :], ALU.add, ALU.mult))
                la(LA_TG)
                stt(halves(g_t[:, :]), halves(g_t[:, :]), 1.0, out(O_LRU + r), ALU.add, ALU.mult).then_inc(s["out_free"], 1)
                la(LA_A2)
                done(stt(l_t2[:, :], l_a2[:, :], 1.0, l_t2[:, :], ALU.add, ALU.mult))
                if not last:
                    lv(LV_IX)
                    lru_front(j + 1)
                la(LA_SQ)
                done(stt(l_u[:, :], t_i[:, :], 0.5, l_u[:, :], ALU.mult, ALU.mult))
                a0, u0 = l_a[:, SEQ:TOK:DEC_L], l_u[:, SEQ:TOK:DEC_L]
                done(dve.tensor_tensor(l_ah[:, :], a0, h0_lru[:, bass.ds(j, 1), :].rearrange("p o b -> p (o b)"), ALU.mult))
                lv(LV_AH)
                done(dve.tensor_tensor(u0, u0, l_ah[:, :], ALU.add))
                done(dve.memset(a0, 0.0))
                lv(LV_A0)
                dve.wait_ge(s["htail_in"], j * 2 + 1)
                done(dve.tensor_tensor_scan(h_seq[:, :], l_a[:, :], l_u[:, :], 0.0, ALU.mult, ALU.add))
                lv(LV_SCAN)
                dve.wait_ge(s["out_free"], j * 2 + (O_LRU + r + 1))
                done(stt(feature_tile(resid, j), g_t[:, :], 0.5, h_seq[:, :], ALU.mult, ALU.mult))

            lru_front(0)
            with dve.Fori(0, KT - 1) as j:
                lru_head(j)
            take(U_DT, O_DT, 1, 1, 0)
            dve.tensor_scalar(halves(dt_x[:, :]), out(O_DT)[0:HEADS], head_vec[:, 0:1], None, ALU.add).then_inc(s["out_free"], 1)
            chained("dt_v", 0, dve.memset(keep[:, :], 1.0), 1)
            chained("dt_v", 0, dve.memset(keep[:, 0:SEQ:P], 0.0), 2)
            chained("dt_v", 0, dve.memset(keep[:, SEQ:TOK:DEC_L], 0.0), 3)
            dve.wait_ge(s["dt_a"], 3)
            chained("dt_v", 0, dve.tensor_scalar(dt_w[:, :], dt_e[:, :], 1.0, None, ALU.add), 4)
            chained("dt_v", 0, dve.tensor_scalar(dt_row[:, :], dt_w[:, :], -1.0, TINY, ALU.add, ALU.add), 5)
            chained("dt_v", 0, dve.reciprocal(dt_row[:, :], dt_row[:, :]), 6)
            dve.wait_ge(s["dt_a"], 4)
            chained("dt_v", 0, stt(dt_l[:, :], dt_l[:, :], TINY, dt_e[:, :], ALU.add, ALU.mult), 7)
            chained("dt_v", 0, dve.tensor_tensor(dt_l[:, :], dt_l[:, :], dt_row[:, :], ALU.mult), 8)
            chained("dt_v", 0, stt(dt_row[:, :], dt_x[:, :], 0.0, dt_l[:, :], ALU.max, ALU.add), 9)
            chained("dt_v", 0, dve.tensor_scalar(head_vec[:, 3:4], head_vec[:, 2:3], -1.0, None, ALU.mult), 10)
            chained("dt_v", 0, dve.tensor_scalar(da_row[:, :], dt_row[:, :], head_vec[:, 3:4], None, ALU.mult), 11)
            chained("dt_v", 0, dve.tensor_tensor_scan(e_row[:, :], keep[:, :], da_row[:, :], 0.0, ALU.mult, ALU.add), 12)
            dve.wait_ge(s["dt_p"], 1)
            chained("dt_v", 0, dve.tensor_copy(dt_col[:, :, :].rearrange("p t h -> p (t h)"), pn[0][:, 0, 0:NT * HEADS]), 13)
            chained("dt_v", 0, dve.tensor_copy(da_col[:, :, :].rearrange("p t h -> p (t h)"), pn[0][:, 0, NT * HEADS:2 * NT * HEADS]), 14)
            dve.wait_ge(s["dt_a"], DT_A)
            chained("dt_v", 0, dve.tensor_tensor(da_lo[:, :, :], da_col[:, :, :], da_hr[:, :, :].bitcast(F32), ALU.subtract), 15)
            chained("dt_v", 0, dve.tensor_tensor(dd_col[:, :, :], dd_col[:, :, :], dt_col[:, :, :], ALU.mult), 16)

            lru_head(KT - 1, True)

            with dve.Fori(0, GROUPS) as g:
                def done(ins):
                    ins.then_inc(s["ssd_v"], 1)

                def sp_(t, step):
                    dve.wait_ge(s["ssd_p"], g * SP_GRP + (SP * t + step))

                def sa(t, step):
                    dve.wait_ge(s["ssd_a"], g * (SA * NT) + (SA * t + step))

                def sv(t, step):
                    dve.wait_ge(s["ssd_v"], g * SV_GRP + (SV * t + step))

                def per_head(ap):
                    return ap.unsqueeze(2).to_broadcast([P, HPG, HD])

                def silu_z(q):
                    k = UG_Z + q
                    take(U_GRP + k, O_GRP + k, GRP_UNITS, GRP_OUTS, g)
                    dve.wait_ge(s["z_th"], g * PAIRS + (q + 1))
                    stt(halves(sz[:, q, :]), halves(rtmp[:, :]), 1.0, out(O_GRP + k), ALU.add, ALU.mult).then_inc(s["out_free"], 1)

                def gate(f):
                    take(U_GRP + UG_MIX + f, O_GRP + OG_MIX[f], GRP_UNITS, GRP_OUTS, g)
                    dve.wait_ge(s["gate_th"], g * 4 + (f + 1))
                    dve.tensor_scalar(gate_buf[f], gate_buf[f], 1.0, None, ALU.add).then_inc(s["out_free"], 1)

                for k in range(PAIRS + 2):
                    take(U_GRP + k, O_GRP + k, GRP_UNITS, GRP_OUTS, g)
                    c = g * PAIRS + k if k < PAIRS else g + (16 + 4 * (k - PAIRS))
                    convolve(xf[:, k, :], g * 6 + (KT + k), GRP_OUTS, g, O_GRP + k, c + V_SCW, 24, c + V_SCB)
                    dve.wait_ge(s["xb_th"], g * 6 + (k + 1))
                    stt(xf[:, k, :], rtmp[:, :], 1.0, xf[:, k, :], ALU.add, ALU.mult).then_inc(s["xb_out"], 1)
                dve.wait_ge(s["eq_mm"], g + 1)
                dve.tensor_copy(eq[:, :], pn[1][:, 0, 0:PAIRS * (DEC_B + 1)]).then_inc(s["eq_cp"], 1)
                silu_z(0)
                for t in range(NT):
                    tile = slice(t * P, (t + 1) * P)
                    sp_(t, SP_CB)
                    sa(t, SA_BT)
                    done(dve.tensor_tensor(cbm[:, :], pn[0][:, 1, P:2 * P], le_mask[:, t // (NT - 1), :], ALU.mult))
                    x_tok = pn[0][:, 0, :].rearrange("p (h d) -> p h d", h=HPG)
                    done(dve.tensor_tensor(xd[:, :, :], x_tok, per_head(dt_col[:, t, bass.ds(g * HPG, HPG)]), ALU.mult))
                    done(dve.tensor_tensor(xdd[:, :, :], x_tok, per_head(dd_col[:, t, bass.ds(g * HPG, HPG)]), ALU.mult))
                    sa(t, SA_L)
                    sv(t, SV_CBM)
                    done(dve.tensor_tensor(lmat[:, :, :], lmat[:, :, :], cbm[:, :].unsqueeze(1).to_broadcast([P, HPG, P]), ALU.mult))
                    if t < NT - 2:
                        silu_z(t + 1)
                    elif t == NT - 2:
                        gate(0)
                    else:
                        def old_states(qq):
                            for a in range(2):
                                o = O_GRP + OG_OLD[qq] + a
                                dve.wait_ge(s["out_ready"], g * GRP_OUTS + (o + 1))
                                dve.tensor_copy(h0_t[:, a, :, :].rearrange("p (c b) n -> p c (b n)", c=2),
                                                pu[o % 2][:, :, :]).then_inc(s["out_free"], 1)

                        def decay_states(qq):
                            for a in range(2):
                                q = 2 * qq + a
                                dec = eq[:, q * (DEC_B + 1):q * (DEC_B + 1) + DEC_B]
                                dve.tensor_tensor(h0[qq][:, a, :, :], h0[qq][:, a, :, :],
                                                  dec.unsqueeze(2).to_broadcast([P, DEC_B, NS]), ALU.mult).then_inc(s["hs_step"], 1)

                        def new_states(qq):
                            for a in range(2):
                                o = O_GRP + OG_NEW[qq] + a
                                dve.wait_ge(s["out_ready"], g * GRP_OUTS + (o + 1))
                                dve.wait_ge(s["hs_step"], g * 4 + (2 * qq + a + 1))
                                hv = h0[qq][:, a, :, :].rearrange("p (c b) n -> p c (b n)", c=2)
                                dve.tensor_tensor(hv, hv, pu[o % 2][:, :, :], ALU.add).then_inc(s["out_free"], 1)

                        old_states(0)
                        decay_states(0)
                        sv(NT - 2, SV_Y)
                        for q in range(PAIRS):
                            dve.tensor_tensor(xf[:, q, 0:SEQ], xf[:, q, 0:SEQ], sz[:, q, 0:SEQ], ALU.mult).then_inc(s["yz"], 1)
                        clear_sum(g + 2)
                        for q in range(PAIRS):
                            add_square(g * SQG + (SQ_GRP + q), q % 2, SEQ)
                        gate(1)
                        old_states(1)
                        new_states(0)
                        decay_states(1)
                        new_states(1)
                    sp_(t, SP_YO)
                    sa(t, SA_ES)
                    yv = y_t[:, :, :].rearrange("p q l -> p (q l)")
                    done(dve.tensor_tensor(yv, pn[0][:, 1, :], es[:, :], ALU.mult))
                    sv(t, SV_T1)
                    done(dve.tensor_tensor(yv, yv, pn[0][:, 0, :], ALU.add))
                    sv(t, SV_T2)
                    if t < NT - 1:
                        done(dve.tensor_tensor(ht[:, :, :], ht[:, :, :], per_head(e_tot[:, t, bass.ds(g * HPG, HPG)]), ALU.mult))
                        sv(t, SV_H0)
                        sp_(t, SP_ST)
                        hv = ht[:, :, :].rearrange("p h d -> p (h d)")
                        done(dve.tensor_tensor(hv, hv, pn[1][:, 1, :], ALU.add))
                    for q in range(PAIRS):
                        c = q * (DEC_B + 1) + DEC_B
                        ins = stt(xf[:, q, tile], xf[:, q, tile], eq[:, c:c + 1], y_t[:, q, :], ALU.mult, ALU.add)
                    done(ins)
                    if t == NT - 2:
                        dve.wait_ge(s["hp_mm"], g + 1)
                        dve.tensor_copy(hp_rows[:, :, :].rearrange("p q n -> p (q n)"), pn[1][:, 1, :]).then_inc(s["hp_cp"], 1)
                sv(NT - 1, SV_Y_LAST)
                ys = xf[:, 0:PAIRS, SEQ:TOK]
                dve.tensor_tensor(ys, ys, sz[:, :, SEQ:TOK], ALU.mult).then_inc(s["yz"], 1)
                dve.wait_ge(s["sq_done"], g * SQG + (SQ_GRP + SQG))
                sampled_sum = rvar[:, SEQ:TOK]
                for q in range(PAIRS):
                    ins = dve.tensor_tensor(sampled_sum, sampled_sum, squares[:, 0, q * P:(q + 1) * P], ALU.add)
                    if q < PAIRS - 1:
                        ins.then_inc(s["sq_part"], 1)
                        dve.wait_ge(s["sq_part"], g * (PAIRS - 1) + (q + 1))
                    else:
                        ins.then_inc(s["sq_added"], 1)
                gate(2)
                norm(g + 2, g * PAIRS + XN_GRP, xf, PAIRS, 0.25 / 512, lambda k: g * PAIRS + (V_SNG + k), yn_hi, yn_lo)
                gate(3)
                dve.wait_ge(s["acc_zero"], 1)
                for r in range(4):
                    for m in range(2):
                        o = O_GRP + OG_BR + 2 * r + m
                        if m == 1:
                            cut_weights(U_GRP + UG_BR + 2 + r, GRP_UNITS, g)
                        dve.wait_ge(s["out_ready"], g * GRP_OUTS + (o + 1))
                        acc = halves(acc_ssd[:, 2 * r + m, :])
                        dve.tensor_tensor(acc, acc, out(o), ALU.add).then_inc(s["out_free"], 1)

            for k in range(2):
                dve.memset(m_a[:, k:k + 1], 0.0).then_inc(s["mg_v"], 1)
            for k in range(KT):
                dve.wait_ge(s["yl_hi_done"], k + 1)
                dve.tensor_tensor(yl_lo[:, k, :], resid[:, k, :], yl_hi[:, k, :].bitcast(F32), ALU.subtract).then_inc(s["yl_lo_done"], 1)
            dve.wait_ge(s["yl_lo_done"], KT)
            with dve.Fori(0, KT // 2) as i:
                for m in range(2):
                    dve.wait_ge(s[f"gate_in{m}"], i * 16 + 16)
                    dve.wait_ge(s["mg_v"], i * 2 + (m + 2))
                    dve.tensor_tensor(m_b[:, :], gates[:, m, TOK:], feature_tile(acc_ssd, i * 2 + m), ALU.mult).then_inc(s["mg_b"], 1)
                    take(U_MRG + m, O_MRG + m, 2, 2, i)
                    dve.tensor_tensor(halves(m_a[:, :]), halves(gates[:, m, 0:TOK]), out(O_MRG + m), ALU.mult).then_inc(s["out_free"], 1)
                    dve.wait_ge(s["out_free"], i * 2 + (O_MRG + m + 1))
                    dve.wait_ge(s["mg_b"], i * 2 + (m + 1))
                    dve.tensor_tensor(feature_tile(resid, i * 2 + m), m_a[:, :], m_b[:, :], ALU.add).then_inc(s["mg_v"], 1)
                    dve.wait_ge(s["mh_done"], i * 2 + (m + 1))
                    dve.tensor_tensor(feature_tile(act_lo, i * 2 + m), feature_tile(resid, i * 2 + m),
                                      feature_tile(act_hi, i * 2 + m).bitcast(F32), ALU.subtract).then_inc(s["ml_done"], 1)
            for a in range(5):
                o = O_TAIL + a
                dve.wait_ge(s["out_ready"], o + 1)
                dst, rows_ = (tail_rows[:, a * D_MODEL:(a + 1) * D_MODEL], TAIL) if a < 4 else (htail_rows[:, :], 1 + DEC_B)
                dve.tensor_copy(dst.rearrange("p (b c) -> p b c", b=2), pu[o % 2][0:rows_, :, :]).then_inc(s["out_free"], 1)
            dve.wait_ge(s["reload"], 16)
            dve.wait_ge(s["ml_done"], KT)
            clear_sum(2 + GROUPS)
            with dve.Fori(0, KT // 2) as i:
                for k in range(2):
                    take(U_OUT + k, O_OUT + k, 2, 2, i)
                    stt(halves(feature_tile(resid, i * 2 + k)), out(O_OUT + k), 0.5,
                        halves(feature_tile(x_res, i * 2 + k)), ALU.mult, ALU.add).then_inc(s["out_free"], 1)
                    add_square(i * 2 + (SQ_FFN2 + k), k)
            ffn(U_FFN2, O_FFN2, 22, 2 + GROUPS, XN_FFN2, V_NF2, True)

            dve.wait_ge(s["gfin"], 16)
            for t in range(NT):
                f = [fin[:, k, t:t + 1] for k in range(8)]
                dve.wait_ge(s["fin_a"], 2 * t + 1)
                chained("fin_v", 6 * t, dve.tensor_scalar(f[1], f[0], 1.0 / D_MODEL, EPS, ALU.mult, ALU.add), 1)
                dve.wait_ge(s["fin_a"], 2 * t + 2)
                chained("fin_v", 6 * t, dve.reciprocal(f[3], f[2]), 2)
                chained("fin_v", 6 * t, dve.tensor_tensor(f[4], f[1], f[3], ALU.mult), 3)
                chained("fin_v", 6 * t, dve.tensor_tensor(f[4], f[4], f[3], ALU.mult), 4)
                chained("fin_v", 6 * t, dve.tensor_scalar(f[4], f[4], -0.5, 1.5, ALU.mult, ALU.add), 5)
                chained("fin_v", 6 * t, dve.tensor_tensor(f[5], f[3], f[4], ALU.mult), 6)
                if t >= 2:
                    dve.wait_ge(s["y_dma"], 16 * (t - 1))
                stt(y_out[:, t % 2, :].rearrange("p (b c) -> p b c", b=2), pu[(O_FIN + t) % 2][:, :, :], f[5],
                    g_fin[:, :].rearrange("p (b c) -> p b c", b=2), ALU.mult, ALU.mult).then_inc(s["out_free"], 1)


_INS = ['x_prompt', 'x_sample', 'state_lru_conv', 'state_lru_h', 'state_ssd_conv', 'state_ssd_h',
        'norm_ffn1_g', 'ffn1_w_up', 'ffn1_w_down', 'norm_mix_g', 'w_in', 'b_gate',
        'lru_conv_w', 'lru_conv_b', 'lru_w_rg', 'lru_b_rg', 'lru_w_ig', 'lru_b_ig', 'lru_lambda',
        'ssd_conv_w', 'ssd_conv_b', 'ssd_dt_bias', 'ssd_A_log', 'ssd_D', 'ssd_norm_g',
        'w_br_lru', 'w_br_ssd', 'w_out', 'norm_ffn2_g', 'ffn2_w_up', 'ffn2_w_down', 'norm_final_g']
_OUTS = [(1, SEQ, D_MODEL), (DEC_B, DEC_L, D_MODEL),
         (1, 1, HIST, D_MODEL), (1, 1, D_MODEL), (1, 1, HIST, 24 * P), (1, 1, HEADS, HD, NS),
         (1, DEC_B, HIST, D_MODEL), (1, DEC_B, D_MODEL), (1, DEC_B, HIST, 24 * P), (1, DEC_B, HEADS, HD, NS)]


def kernel(**inputs):
    import numpy as _np
    import concourse.bacc as _bacc
    from concourse import mybir as _mybir
    from concourse.bass_utils import run_bass_kernel_spmd as _run

    nc = _bacc.Bacc("TRN2", target_bir_lowering=False, num_devices=1)
    arrays, args = {}, []
    for name in _INS:
        a = _np.ascontiguousarray(inputs[name])
        arrays[f"in_{name}_dram"] = a
        args.append(nc.dram_tensor(f"in_{name}_dram", a.shape, _mybir.dt.from_np(a.dtype), kind="ExternalInput").ap())
    for i, shape in enumerate(_OUTS):
        args.append(nc.dram_tensor(f"out_{i}_dram", shape, _mybir.dt.float32, kind="ExternalOutput").ap())
    layer(nc, *args)
    r = _run(nc, [arrays], core_ids=[0])
    return tuple(r.results[0][f"out_{i}_dram"] for i in range(len(_OUTS)))
```
